# Optimizing a Trainium2 kernel written in Bass

```python
import jax, jax.numpy as jnp
from jax import lax
import numpy as np

D_MODEL = 1024
BATCH = 1
SEQ = 2048
DEPTH = 1

CHUNK = 64
QBLOCK = 128
EPS = 1e-6

D_MIX_A = D_MODEL
HGRN_EXPAND = 128
HGRN_HEADS = D_MIX_A // HGRN_EXPAND
HGRN_DK = HGRN_EXPAND
HGRN_DV = D_MIX_A // HGRN_HEADS
D_MIX_B = D_MODEL
SB_HEAD_DIM = 64
SB_HEADS = D_MIX_B // SB_HEAD_DIM
D_MIX = D_MIX_A + D_MIX_B

IN_WIDTHS = (HGRN_HEADS * HGRN_DK, HGRN_HEADS * HGRN_DK, D_MIX_A, D_MIX_A,
             D_MIX_B, D_MIX_B, D_MIX_B, D_MIX_B)
D_IN = sum(IN_WIDTHS)
IN_OFFSETS = tuple(int(v) for v in np.cumsum(IN_WIDTHS)[:-1])

kernel_name = "hybrid_hgrn2_stickbreaking_adaln_trunk"

def rms_norm(x, g):
    xf = x.astype(jnp.float32)
    y = xf * lax.rsqrt(jnp.mean(xf * xf, axis=-1, keepdims=True) + EPS)
    return (y * g.astype(jnp.float32)).astype(x.dtype)

def hgrn2_mixer(q, f_logit, i, lb):
    bsz, seq = q.shape[0], q.shape[1]
    n_chunks = seq // CHUNK
    q = jax.nn.silu(q.astype(jnp.float32))
    fl = f_logit.astype(jnp.float32)
    lb = lb.astype(jnp.float32)
    log_f = jnp.logaddexp(jnp.log(lb), jnp.log1p(-lb) + jax.nn.log_sigmoid(fl))
    k = (1.0 - lb) * jax.nn.sigmoid(-fl)

    def to_chunks(t, d):
        return t.reshape(bsz, n_chunks, CHUNK, HGRN_HEADS, d).transpose(1, 0, 3, 2, 4)

    qc = to_chunks(q, HGRN_DK)
    kc = to_chunks(k, HGRN_DK)
    ic = to_chunks(i.astype(jnp.float32), HGRN_DV)
    bc = jnp.cumsum(to_chunks(log_f, HGRN_DK), axis=3)
    causal = jnp.tril(jnp.ones((CHUNK, CHUNK), dtype=bool))[:, :, None]

    def step(state, xs):
        q_, k_, i_, b_ = xs
        diff = b_[:, :, :, None, :] - b_[:, :, None, :, :]
        decay = jnp.where(causal, jnp.exp(jnp.where(causal, diff, 0.0)), 0.0)
        scores = jnp.einsum('bhtd,bhsd,bhtsd->bhts', q_, k_, decay)
        b_last = b_[:, :, -1, :]
        o = (jnp.einsum('bhts,bhsv->bhtv', scores, i_)
             + jnp.einsum('bhtd,bhdv->bhtv', q_ * jnp.exp(b_), state))
        k_dec = k_ * jnp.exp(b_last[:, :, None, :] - b_)
        state = jnp.exp(b_last)[..., None] * state + jnp.einsum('bhsd,bhsv->bhdv', k_dec, i_)
        return state, o

    s0 = jnp.zeros((bsz, HGRN_HEADS, HGRN_DK, HGRN_DV), jnp.float32)
    _, o = lax.scan(step, s0, (qc, kc, ic, bc))
    return o.transpose(1, 0, 3, 2, 4).reshape(bsz, seq, HGRN_HEADS, HGRN_DV)

def stick_breaking_attention(q, k, v):
    seq = q.shape[1]
    scale = SB_HEAD_DIM ** -0.5
    qh = q.astype(jnp.float32).transpose(0, 2, 1, 3)
    kh = k.astype(jnp.float32).transpose(0, 2, 1, 3)
    vh = v.astype(jnp.float32).transpose(0, 2, 1, 3)
    outs = []
    for nb in range(seq // QBLOCK):
        t0, t1 = nb * QBLOCK, (nb + 1) * QBLOCK
        z = jnp.einsum('bhtd,bhsd->bhts', qh[:, :, t0:t1], kh[:, :, :t1]) * scale
        mask = jnp.arange(t1)[None, :] < (t0 + jnp.arange(QBLOCK))[:, None]
        log_keep = jnp.where(mask, jax.nn.log_sigmoid(-z), 0.0)
        rc = lax.cumsum(log_keep, axis=3, reverse=True)
        after = jnp.concatenate([rc[..., 1:], jnp.zeros_like(rc[..., :1])], axis=-1)
        w = jnp.where(mask, jnp.exp(jax.nn.log_sigmoid(z) + after), 0.0)
        outs.append(jnp.einsum('bhts,bhsd->bhtd', w, vh[:, :, :t1]))
    o = jnp.concatenate(outs, axis=2)
    return o.transpose(0, 2, 1, 3)

def setup_inputs(seed: int = 0) -> dict:
    key = jax.random.key(seed)
    ks = jax.random.split(key, 12)
    f32 = jnp.float32
    x = jax.random.normal(ks[0], (BATCH, SEQ, D_MODEL), f32)
    c = jax.random.normal(ks[1], (BATCH, D_MODEL), f32)
    w_ada = jax.random.normal(ks[2], (DEPTH, D_MODEL, 3 * D_MODEL), f32) * (0.5 * D_MODEL ** -0.5)
    b_ada = jax.random.normal(ks[3], (DEPTH, 3 * D_MODEL), f32) * 0.01
    norm_g = 1.0 + 0.01 * jax.random.normal(ks[4], (DEPTH, D_MODEL), f32)
    w_in = jax.random.normal(ks[5], (DEPTH, D_MODEL, D_IN), f32) * D_MODEL ** -0.5
    lb_logits = jax.random.normal(ks[6], (DEPTH, HGRN_HEADS * HGRN_DK), f32)
    hgrn_norm_g = 1.0 + 0.01 * jax.random.normal(ks[7], (DEPTH, HGRN_DV), f32)
    sb_norm_g = 1.0 + 0.01 * jax.random.normal(ks[8], (DEPTH, SB_HEAD_DIM), f32)
    w_out = jax.random.normal(ks[9], (DEPTH, D_MIX, D_MODEL), f32) * D_MIX ** -0.5
    final_g = 1.0 + 0.01 * jax.random.normal(ks[10], (D_MODEL,), f32)
    return {"x": x, "c": c, "w_ada": w_ada, "b_ada": b_ada, "norm_g": norm_g,
            "w_in": w_in, "lb_logits": lb_logits, "hgrn_norm_g": hgrn_norm_g,
            "sb_norm_g": sb_norm_g, "w_out": w_out, "final_g": final_g}

def reference(x, c, w_ada, b_ada, norm_g, w_in, lb_logits, hgrn_norm_g, sb_norm_g, w_out, final_g):
    bsz, seq = x.shape[0], x.shape[1]
    lb_cum = jnp.cumsum(jax.nn.softmax(lb_logits.astype(jnp.float32), axis=0), axis=0)
    lower_bounds = lb_cum - lb_cum[0:1]
    c_act = jax.nn.silu(c)
    for layer in range(DEPTH):
        mod = c_act @ w_ada[layer] + b_ada[layer]
        shift, scale, gate = jnp.split(mod, 3, axis=-1)
        h = rms_norm(x, norm_g[layer]) * (1.0 + scale[:, None, :]) + shift[:, None, :]
        u = h @ w_in[layer]
        a_q, a_f, a_i, a_g, b_q, b_k, b_v, b_g = jnp.split(u, IN_OFFSETS, axis=-1)
        o_a = hgrn2_mixer(a_q, a_f, a_i, lower_bounds[layer])
        o_a = rms_norm(o_a, hgrn_norm_g[layer]).reshape(bsz, seq, D_MIX_A)
        o_a = (o_a * jax.nn.silu(a_g.astype(jnp.float32))).astype(x.dtype)
        o_b = stick_breaking_attention(b_q.reshape(bsz, seq, SB_HEADS, SB_HEAD_DIM),
                                       b_k.reshape(bsz, seq, SB_HEADS, SB_HEAD_DIM),
                                       b_v.reshape(bsz, seq, SB_HEADS, SB_HEAD_DIM))
        o_b = rms_norm(o_b, sb_norm_g[layer]).reshape(bsz, seq, D_MIX_B)
        o_b = (o_b * jax.nn.silu(b_g.astype(jnp.float32))).astype(x.dtype)
        y = jnp.concatenate([o_a, o_b], axis=-1) @ w_out[layer]
        x = x + gate[:, None, :] * y
    return rms_norm(x, final_g)


_drawn_inputs = setup_inputs


def setup_inputs(seed=0):
    import zlib

    import numpy as np

    out = dict(_drawn_inputs(seed))
    spreads = {}
    factors = {'b_ada': 7.178, 'norm_g': 8.0, 'hgrn_norm_g': 8.0, 'sb_norm_g': 8.0, 'final_g': 5.845}
    for name, (base, spread) in spreads.items():
        noise = np.random.default_rng([zlib.crc32(name.encode()), seed]).standard_normal(out[name].shape)
        drawn = base * np.exp(spread * noise) if base else spread * noise
        out[name] = __import__('jax').numpy.asarray(drawn.astype(out[name].dtype))
    for name, factor in factors.items():
        out[name] = (out[name] * factor).astype(out[name].dtype)
    return out
```

```python
from contextlib import ExitStack

import concourse.bass as bass
from concourse import mybir

F32 = mybir.dt.float32
F32R = mybir.dt.float32r
I32 = mybir.dt.int32
ALU = mybir.AluOpType
ACT = mybir.ActivationFunctionType
AX = mybir.AxisListType

P = 128
D = 1024
SEQ = 2048
KD = D // P
TB = SEQ // P
TG = SEQ // 512
EPS = 1e-6
GH = 8
GD = 128
SH = 16
SD = 64
NHEAD = GH + SH
WC = 256
NCH = 8 * D // WC
CH_T = D // WC
KO = 2 * D // P
NLEV = 8
NPRED = 6


class Mem:

    def __init__(self, nc, stack):
        self.nc, self.stack = nc, stack

    def sb(self, name, shape, dt=F32):
        return self.stack.enter_context(self.nc.sbuf_tensor(name, shape, dt))

    def ps(self, name, shape):
        return self.stack.enter_context(self.nc.psum_tensor(name, shape, F32))

    def sem(self, name):
        return self.stack.enter_context(self.nc.semaphore(name))


def condition(nc, io, keep, h_hi, h_lo):
    with ExitStack() as stack:
        m = Mem(nc, stack)
        AC = 256
        n_ada = 3 * D // AC
        ada = m.sb("ada", [P, 2, KD, AC])
        xg = m.sb("xg", [P, 2, 4, D])
        c_act = m.sb("c_act", [P, KD, P])
        small = m.sb("small", [P, 5, KD])
        c_sig = m.sb("c_sig", [P, KD])
        c_col = m.sb("c_col", [P, KD])
        mod = m.sb("mod", [P, 2, KD, P])
        mod_col = m.sb("mod_col", [P, 2, KD])
        shift = m.sb("shift", [P, KD])
        mul = m.sb("mul", [P, KD])
        lb_tmp = m.sb("lb_tmp", [P, 3, GH])
        stat = m.sb("stat", [P, 5, 4])
        hx = m.sb("hx", [P, 2, 512])
        mod_ps = [m.ps(f"mod_ps{i}", [P, 512]) for i in range(2)]
        xt_ps = [m.ps(f"xt_ps{i}", [P, 512]) for i in range(4)]
        junk = m.ps("junk", [P, D])

        ada_in = [m.sem(f"ada_in{i}") for i in range(2)]
        x_in = [m.sem(f"x_in{i}") for i in range(2)]
        small_in = m.sem("small_in")
        act_small = m.sem("act_small")
        cb_ready = m.sem("cb_ready")
        mod_ready = m.sem("mod_ready")
        mod_taken = m.sem("mod_taken")
        sq_ready = m.sem("sq_ready")
        var_ready = m.sem("var_ready")
        root_ready = m.sem("root_ready")
        xn_ready = m.sem("xn_ready")
        xt_ready = m.sem("xt_ready")
        col_ready = m.sem("col_ready")
        hi_ready = m.sem("hi_ready")
        hx_ready = m.sem("hx_ready")
        lo_ready = m.sem("lo_ready")
        dve_step = m.sem("dve_step")
        n_small = 9

        with nc.Block() as block:
            @block.sync
            def _(sp):
                def load_ada(n):
                    if n >= 2:
                        sp.wait_ge(mod_ready, n - 1)
                    sp.dma_start(ada[:, n % 2], io["w_ada"][n]).then_inc(ada_in[n % 2], 16)

                def load_x(g):
                    if g >= 2:
                        sp.wait_ge(xt_ready, KD * (g - 1))
                    src = io["x"][g * 512:(g + 1) * 512, :].rearrange("(b p) n -> p b n", p=P)
                    sp.dma_start(xg[:, g % 2], src).then_inc(x_in[g % 2], 16)

                load_ada(0)
                load_ada(1)
                load_x(0)
                load_ada(2)
                load_ada(3)
                load_x(1)
                for n in range(4, n_ada):
                    load_ada(n)
                load_x(2)
                load_x(3)

            @block.tensor
            def _(pe):
                pe.wait_ge(cb_ready, 1)
                for n in range(n_ada):
                    pe.wait_ge(ada_in[n % 2], 16 * (n // 2 + 1))
                    if n >= 2:
                        pe.wait_ge(mod_taken, n - 1)
                    for k in range(KD):
                        mm = nc.tensor.matmul(mod_ps[n % 2][:, 0:AC], c_act[:, k, :], ada[:, n % 2, k, :],
                                              start=(k == 0), stop=(k == KD - 1))
                    mm.then_inc(mod_ready, 1)
                for g in range(TG):
                    pe.wait_ge(xn_ready, 4 * (g + 1))
                    for k in range(KD):
                        n = g * KD + k
                        if n >= 4:
                            pe.wait_ge(hx_ready, n - 3)
                        for b in range(4):
                            mm = nc.tensor.transpose(xt_ps[n % 4][:, b * P:(b + 1) * P],
                                                     xg[:, g % 2, b, k * P:(k + 1) * P], keep["ident"][:, :])
                        mm.then_inc(xt_ready, 1)

            @block.scalar
            def _(act):
                act.dma_start(small[:, :, :], io["small"]).then_inc(small_in, 16)
                act.dma_start(keep["ident"][:, :], io["ident"]).then_inc(small_in, 16)
                act.dma_start(keep["gate"][:, :], io["b_gate"].partition_broadcast(P)).then_inc(small_in, 16)
                act.dma_start(keep["g_hgrn"][:, :], io["g_hgrn"].partition_broadcast(P)).then_inc(small_in, 16)
                act.dma_start(keep["g_stick"][:, :], io["g_stick"].partition_broadcast(P)).then_inc(small_in, 16)
                act.wait_ge(small_in, 80)
                nc.scalar.activation(c_sig[:, :], small[:, 0, :], ACT.Sigmoid).then_inc(act_small, 1)
                act.wait_ge(dve_step, 1)
                nc.scalar.activation(lb_tmp[:, 1, :], lb_tmp[:, 0, :], ACT.Exp).then_inc(act_small, 1)
                for g in range(TG):
                    act.wait_ge(x_in[g % 2], 16 * (g // 2 + 1))
                    if g >= 1:
                        act.wait_ge(var_ready, g)
                    for b in range(4):
                        if g or b:
                            act.wait_ge(sq_ready, 4 * g + b)
                        nc.scalar.activation(junk[:, :], xg[:, g % 2, b, :], ACT.Square,
                                             accum_out=stat[:, 0, b:b + 1]).then_inc(sq_ready, 1)
                    act.wait_ge(var_ready, g + 1)
                    nc.scalar.activation(stat[:, 2, :], stat[:, 1, :], ACT.Sqrt).then_inc(root_ready, 1)
                    if g == 0:
                        act.wait_ge(col_ready, 1)
                    for k in range(KD):
                        n = g * KD + k
                        act.wait_ge(xt_ready, n + 1)
                        nc.scalar.activation(h_hi[:, k, g * 512:(g + 1) * 512], xt_ps[n % 4][:, :], ACT.Identity,
                                             bias=shift[:, k:k + 1], scale=mul[:, k:k + 1]).then_inc(hi_ready, 1)

            @block.vector
            def _(dve):
                done = [0]

                def step(ins):
                    done[0] += 1
                    ins.then_inc(dve_step, 1)
                    dve.wait_ge(dve_step, done[0])

                dve.wait_ge(small_in, 80)
                step(nc.vector.tensor_tensor(lb_tmp[:, 0, :], small[:, 4, :], small[:, 4, :], ALU.subtract))
                dve.wait_ge(act_small, 1)
                step(nc.vector.tensor_tensor(c_col[:, :], small[:, 0, :], c_sig[:, :], ALU.mult))
                nc.vector.tensor_copy(c_act[:, :, :], c_col[:, :].unsqueeze(2).to_broadcast([P, KD, P])).then_inc(cb_ready, 1)
                dve.wait_ge(act_small, 2)
                step(nc.vector.reciprocal(lb_tmp[:, 2, :], lb_tmp[:, 1, :]))
                step(nc.vector.tensor_tensor(lb_tmp[:, 2, :], lb_tmp[:, 2, :], lb_tmp[:, 1, :], ALU.mult))
                step(nc.vector.tensor_tensor(keep["lb"][:, 0, :], lb_tmp[:, 2, :], lb_tmp[:, 2, :], ALU.subtract))
                step(nc.vector.tensor_scalar(keep["lb"][:, 1, :], keep["lb"][:, 0, :], -1.0, 1.0, ALU.mult, ALU.add))

                def norm(g):
                    dve.wait_ge(sq_ready, 4 * (g + 1))
                    v, root, y, a = (stat[:, j, :] for j in (1, 2, 3, 4))
                    nc.vector.tensor_scalar(v, stat[:, 0, :], 1.0 / D, EPS, ALU.mult, ALU.add).then_inc(var_ready, 1)
                    dve.wait_ge(root_ready, g + 1)
                    step(nc.vector.reciprocal(y, root))
                    step(nc.vector.tensor_tensor(a, y, y, ALU.mult))
                    step(nc.vector.tensor_tensor(a, a, v, ALU.mult))
                    step(nc.vector.tensor_scalar(a, a, -0.5, 1.5, ALU.mult, ALU.add))
                    step(nc.vector.tensor_tensor(y, y, a, ALU.mult))
                    for b in range(4):
                        nc.vector.tensor_scalar(xg[:, g % 2, b, :], xg[:, g % 2, b, :], stat[:, 3, b:b + 1], None,
                                                ALU.mult).then_inc(xn_ready, 1)

                def take_mod(n):
                    dve.wait_ge(mod_ready, n + 1)
                    if n < 2 * CH_T:
                        dst = mod[:, n // CH_T, 2 * (n % CH_T):2 * (n % CH_T) + 2, :]
                        nc.vector.tensor_copy(dst, mod_ps[n % 2][:, 0:AC].rearrange("p (a n) -> p a n", a=2)).then_inc(mod_taken, 1)
                    else:
                        dst = keep["gate"][:, (n - 2 * CH_T) * AC:(n - 2 * CH_T + 1) * AC]
                        nc.vector.tensor_tensor(dst, mod_ps[n % 2][:, 0:AC], dst, ALU.add).then_inc(mod_taken, 1)

                norm(0)
                for n in range(2 * CH_T):
                    take_mod(n)
                dve.wait_ge(mod_taken, 2 * CH_T)
                for j in range(2):
                    step(nc.vector.tensor_tensor(mod[:, j], mod[:, j], keep["ident"][:, :].unsqueeze(1).to_broadcast([P, KD, P]),
                                                 ALU.mult))
                    step(nc.vector.tensor_reduce(mod_col[:, j, :], mod[:, j], AX.X, ALU.add))
                step(nc.vector.tensor_tensor(shift[:, :], mod_col[:, 0, :], small[:, 1, :], ALU.add))
                step(nc.vector.tensor_tensor(mod_col[:, 1, :], mod_col[:, 1, :], small[:, 2, :], ALU.add))
                step(nc.vector.tensor_scalar(mod_col[:, 1, :], mod_col[:, 1, :], 1.0, None, ALU.add))
                nc.vector.tensor_tensor(mul[:, :], mod_col[:, 1, :], small[:, 3, :], ALU.mult).then_inc(col_ready, 1)
                for n in range(2 * CH_T, n_ada):
                    take_mod(n)
                dve.wait_ge(col_ready, 1)
                for g in range(TG):
                    for k in range(KD):
                        n = g * KD + k
                        dve.wait_ge(hi_ready, n + 1)
                        if n >= 2:
                            dve.wait_ge(lo_ready, n - 1)
                        nc.vector.tensor_scalar(hx[:, n % 2, :], xt_ps[n % 4][:, :], mul[:, k:k + 1], shift[:, k:k + 1],
                                                ALU.mult, ALU.add).then_inc(hx_ready, 1)
                    if g + 1 < TG:
                        norm(g + 1)

            @block.gpsimd
            def _(pool):
                for n in range(TG * KD):
                    g, k = n // KD, n % KD
                    pool.wait_ge(hx_ready, n + 1)
                    hi = h_hi[:, k, g * 512:(g + 1) * 512].bitcast(F32)
                    nc.gpsimd.tensor_tensor(h_lo[:, k, g * 512:(g + 1) * 512], hx[:, n % 2, :], hi,
                                            ALU.subtract).then_inc(lo_ready, 1)


PROJ = [("gq", True, 0), ("gf", True, 1), ("sq", True, 4), ("sk", True, 5),
        ("gi", False, 2), ("gg", False, 3), ("sv", False, 6), ("sg", False, 7)]


def project(nc, io, keep, h_hi, h_lo, scr):
    with ExitStack() as stack:
        m = Mem(nc, stack)
        w_raw = m.sb("w_raw", [P, KD, WC])
        w_hi = m.sb("w_hi", [P, 2, KD, WC], F32R)
        w_lo = m.sb("w_lo", [P, 2, KD, WC], F32R)
        st = m.sb("st", [P, 2, 512])
        st2 = m.sb("st2", [P, 2, 512])
        st_hi = m.sb("st_hi", [P, 2, 512], F32R)
        st_lo = m.sb("st_lo", [P, 2, 512], F32R)
        sg = m.sb("sg", [P, 2, 512])
        sg2 = m.sb("sg2", [P, 2, 512])
        u_ps = [m.ps(f"u_ps{i}", [P, 512]) for i in range(8)]

        w_in_sem = m.sem("w_loaded")
        w_split = m.sem("w_split")
        u_ready = m.sem("u_ready")
        u_act = m.sem("u_act")
        u_taken = m.sem("u_taken")
        g_step = m.sem("g_step")
        staged = m.sem("staged")
        stored = [m.sem(f"stored{i}") for i in range(2)]
        passed = m.sem("w_passed")
        n_pair = NCH // 2

        def tiles():
            return [(par, j) for par in range(2) for j in range(8)]

        with nc.Block() as block:
            @block.gpsimd
            def _(pool):
                def chunk(c, par):
                    pool.wait_ge(w_in_sem, 16 * c + 16)
                    pool.wait_ge(u_ready, 8 * c + 8)
                    nc.gpsimd.sem_inc(passed, 1)
                    nc.gpsimd.tensor_copy(w_hi[:, par], w_raw[:, :, :]).then_inc(w_split, 1)
                    pool.wait_ge(w_split, 2 * c + 1)
                    nc.gpsimd.tensor_tensor(w_lo[:, par], w_raw[:, :, :], w_hi[:, par].bitcast(F32),
                                            ALU.subtract).then_inc(w_split, 1)

                with nc.gpsimd.Fori(0, n_pair) as i:
                    for par in range(2):
                        chunk(i * 2 + par, par)

            @block.tensor
            def _(pe):
                nc.tensor.sem_inc(u_ready, 16)

                def tile(c, j, par, feature):
                    pe.wait_ge(u_taken, 8 * c + j + 1)
                    if feature:
                        cg, tp = j // 4, j % 4
                        n = 0
                        for wt, ht in ((w_hi, h_hi), (w_hi, h_lo), (w_lo, h_hi)):
                            for k in range(KD):
                                mm = nc.tensor.matmul(u_ps[j][:, :], wt[:, par, k, cg * P:(cg + 1) * P],
                                                      ht[:, k, tp * 512:(tp + 1) * 512], start=(n == 0), stop=(n == 3 * KD - 1))
                                n += 1
                    else:
                        for b in range(2):
                            tb = 2 * j + b
                            n = 0
                            for wt, ht in ((w_hi, h_hi), (w_hi, h_lo), (w_lo, h_hi)):
                                for k in range(KD):
                                    mm = nc.tensor.matmul(u_ps[j][:, b * WC:(b + 1) * WC], ht[:, k, tb * P:(tb + 1) * P],
                                                          wt[:, par, k, :], start=(n == 0), stop=(n == 3 * KD - 1))
                                    n += 1
                    mm.then_inc(u_ready, 1)

                for half, feature in ((0, True), (1, False)):
                    with nc.tensor.Fori(half * n_pair // 2, (half + 1) * n_pair // 2) as i:
                        for par in range(2):
                            c = i * 2 + par
                            pe.wait_ge(w_split, 2 * c + 2)
                            for j in range(8):
                                tile(c, j, par, feature)

            @block.scalar
            def _(act):
                for t, (name, feature, _) in enumerate(PROJ):
                    with nc.scalar.Fori(t * CH_T // 2, (t + 1) * CH_T // 2) as i:
                        for par, j in tiles():
                            n = i * 16 + (par * 8 + j)
                            s = j % 2
                            act.wait_ge(u_ready, n + 17)
                            act.wait_ge(u_taken, n + 7)
                            if name in ("sq", "sk"):
                                act.wait_ge(stored[s], i * 256 + 32 * (4 * par + j // 2 + 1))
                                nc.scalar.activation(st_hi[:, s, :], u_ps[j][:, :], ACT.Copy).then_inc(u_act, 1)
                            elif name == "gf":
                                nc.scalar.activation(sg2[:, s, :], u_ps[j][:, :], ACT.Sigmoid, scale=-1.0)
                                nc.scalar.activation(sg[:, s, :], u_ps[j][:, :], ACT.Sigmoid).then_inc(u_act, 1)
                            elif name in ("gi", "sv"):
                                nc.scalar.activation(sg[:, s, :], u_ps[j][:, :], ACT.Copy).then_inc(u_act, 1)
                            else:
                                nc.scalar.activation(sg[:, s, :], u_ps[j][:, :], ACT.Sigmoid).then_inc(u_act, 1)

            @block.vector
            def _(dve):
                nc.vector.sem_inc(u_taken, 8)
                for t, (name, feature, _) in enumerate(PROJ):
                    with nc.vector.Fori(t * CH_T // 2, (t + 1) * CH_T // 2) as i:
                        for par, j in tiles():
                            n = i * 16 + (par * 8 + j)
                            s = j % 2
                            dve.wait_ge(u_act, n + 1)
                            dve.wait_ge(stored[s], i * 256 + 32 * (4 * par + j // 2 + 1))
                            if name == "gq":
                                ins = nc.vector.tensor_tensor(st[:, s, :], u_ps[j][:, :], sg[:, s, :], ALU.mult)
                            elif name == "gf":
                                hd = (i - t * CH_T // 2) * 4 + (par * 2 + j // 4)
                                lb0 = keep["lb"][:, 0, bass.ds(hd, 1)]
                                lb1 = keep["lb"][:, 1, bass.ds(hd, 1)]
                                nc.vector.tensor_scalar(st2[:, s, :], sg2[:, s, :], lb1, None, ALU.mult)
                                ins = nc.vector.tensor_scalar(st[:, s, :], sg[:, s, :], lb1, lb0, ALU.mult, ALU.add)
                            elif name in ("sq", "sk"):
                                ins = nc.vector.tensor_tensor(st_lo[:, s, :], u_ps[j][:, :], st_hi[:, s, :].bitcast(F32), ALU.subtract)
                            elif name in ("gi", "sv"):
                                ins = nc.vector.tensor_copy(st[:, s, :], sg[:, s, :])
                            else:
                                g = keep["g_hgrn" if name == "gg" else "g_stick"]
                                w = GD if name == "gg" else SD
                                g_steps = (t // 2 - 2) * 32
                                nc.vector.tensor_tensor(st2[:, s, :], u_ps[j][:, :], sg[:, s, :], ALU.mult).then_inc(g_step, 1)
                                dve.wait_ge(g_step, (i - t * CH_T // 2) * 16 + (par * 8 + j + 1 + g_steps))
                                ins = nc.vector.tensor_tensor(
                                    st[:, s, :].rearrange("p (a n) -> p a n", n=w), st2[:, s, :].rearrange("p (a n) -> p a n", n=w),
                                    g[:, :].unsqueeze(1).to_broadcast([P, 512 // w, w]), ALU.mult)
                            ins.then_inc(u_taken, 1)

            @block.sync
            def _(sp):
                sp.sem_inc(stored[0], 32)
                sp.sem_inc(stored[1], 32)

                def load_w(c):
                    sp.dma_start(w_raw[:, :, :], io["w_in"][bass.ds(c, 1)].rearrange("a p k n -> p (a k) n")).then_inc(w_in_sem, 16)

                sp.dma_start(w_raw[:, :, :], io["w_in"][0]).then_inc(w_in_sem, 16)
                for t, (name, feature, _) in enumerate(PROJ):
                    dsts = scr[name]

                    def pair(i2, last):
                        i = i2 + t * CH_T // 2
                        for par, j in tiles():
                            n = i * 16 + (par * 8 + j)
                            s = j % 2
                            if j == 1 and not (last and par == 1):
                                sp.wait_ge(w_split, i * 4 + (2 * par + 2))
                                load_w(i * 2 + (par + 1))
                            sp.wait_ge(u_taken, n + 9)
                            cc = i2 * 2 + par
                            srcs = (st_hi, st_lo) if name in ("sq", "sk") else (st, st2) if name == "gf" else (st,)
                            for q, (src, dst) in enumerate(zip(srcs, dsts)):
                                if src in (st_hi, st_lo):
                                    src = src[:, :, :].bitcast(F32)
                                if feature:
                                    to = dst[bass.ds(cc * WC + (j // 4) * P, P), (j % 4) * 512:(j % 4 + 1) * 512]
                                    frm = src[:, s, :]
                                else:
                                    to = dst[2 * j:2 * j + 2, :, bass.ds(cc * WC, WC)].rearrange("b p n -> p b n")
                                    frm = src[:, s, :].rearrange("p (b n) -> p b n", b=2)
                                sp.dma_start(to, frm).then_inc(stored[s], 32 // len(srcs))

                    if t < len(PROJ) - 1:
                        with nc.sync.Fori(0, CH_T // 2) as i2:
                            pair(i2, False)
                    else:
                        for i2 in range(CH_T // 2):
                            pair(i2, i2 == CH_T // 2 - 1)
                sp.wait_ge(stored[0], n_pair * 256 + 32)
                sp.wait_ge(stored[1], n_pair * 256 + 32)


def hgrn(nc, io, keep, scr, o_scr):
    with ExitStack() as stack:
        m = Mem(nc, stack)
        q = m.sb("hq", [P, 2, SEQ])
        k = m.sb("hk", [P, 2, SEQ])
        f = m.sb("hf", [P, 2, SEQ])
        val = m.sb("hi", [P, 2, TB, GD])
        gat = m.sb("hg", [P, 2, TB, GD])
        sc = m.sb("hsc", [P, 2, SEQ])
        kt = m.sb("hkt", [P, 2, TB, GD])
        state = m.sb("hst", [P, 2, TB, GD])
        tot = m.sb("htot", [P, 2, SEQ])
        og = m.sb("hog", [P, 2, TB, GD])
        sqr = m.sb("hsqr", [P, 2, 512])
        mask = m.sb("hmask", [P, NPRED, P], I32)
        ps = [[m.ps(f"hps{e}{b}", [P, 512]) for b in range(4)] for e in range(2)]

        mask_in = m.sem("mask_in")
        loaded = [m.sem(f"h_loaded{e}") for e in range(2)]
        zeroed = m.sem("h_zeroed")
        mm_ready = [m.sem(f"mm_ready{e}") for e in range(2)]
        bank_free = [[m.sem(f"bank_free{e}{b}") for b in range(4)] for e in range(2)]
        q_level = m.sem("q_level")
        k_level = m.sem("k_level")
        sq_ready = m.sem("hsq_ready")
        red_ready = m.sem("hred_ready")
        st_step = m.sem("st_step")
        passed = m.sem("h_passed")
        og_ready = m.sem("og_ready")
        og_stored = [m.sem(f"og_stored{e}") for e in range(2)]
        n_it = GH // 2
        STEPS = 11
        MB = 4 * STEPS
        T_, DS_, O_ = 8, 9, 10

        def tot_at(e, j):
            if j == 0:
                return f[:, e, :]
            lo = SEQ - (SEQ >> (j - 1))
            return tot[:, e, lo:lo + (SEQ >> j)]

        def level_views(t, e, j, side):
            return t[:, e, :].rearrange("p (b s m) -> p b s m", s=2, m=1 << j)[:, :, side, :]

        def pair_tot(e, j, side):
            nb = SEQ >> (j + 1)
            one = tot_at(e, j).rearrange("p (b s) -> p b s", s=2)[:, :, side]
            return one.unsqueeze(2).to_broadcast([P, nb, 1 << j])

        with nc.Block() as block:
            @block.sync
            def _(sp):
                sp.sem_inc(og_stored[0], 16)
                sp.sem_inc(og_stored[1], 16)
                sp.dma_start(mask[:, :, :], io["mask"]).then_inc(mask_in, 16)

                def load(i, e, first):
                    hd = i * 2 + e
                    rows = bass.ds(hd * P, P)
                    if not first:
                        sp.wait_ge(q_level, (i - 1) * (2 * NLEV) + 4)
                        sp.wait_ge(k_level, (i - 1) * (2 * NLEV) + 4)
                    sp.dma_start(f[:, e, :], scr["gf"][0][rows, :]).then_inc(loaded[e], 16)
                    if not first:
                        sp.wait_ge(mm_ready[e], (i - 1) * MB + 4 * (T_ + 1))
                    sp.dma_start(k[:, e, :], scr["gf"][1][rows, :]).then_inc(loaded[e], 16)
                    if not first:
                        sp.wait_ge(mm_ready[e], (i - 1) * MB + MB)
                    cols = bass.ds(hd * GD, GD)
                    sp.dma_start(q[:, e, :], scr["gq"][0][rows, :]).then_inc(loaded[e], 16)
                    sp.dma_start(val[:, e], scr["gi"][0][:, :, cols].rearrange("b p n -> p b n")).then_inc(loaded[e], 16)
                    if not first:
                        sp.wait_ge(og_ready, (i - 1) * 8 + 4 * (e + 1))
                    sp.dma_start(gat[:, e], scr["gg"][0][:, :, cols].rearrange("b p n -> p b n")).then_inc(loaded[e], 16)

                def store(i, e):
                    sp.wait_ge(og_ready, i * 8 + 4 * (e + 1))
                    cols = bass.ds((i * 2 + e) * GD, GD)
                    sp.dma_start(o_scr[:, :, cols].rearrange("b p n -> p b n"), og[:, e]).then_inc(og_stored[e], 16)

                load(0, 0, True)
                load(0, 1, True)
                with nc.sync.Fori(0, n_it - 1) as j:
                    for e in range(2):
                        load(j + 1, e, False)
                        store(j, e)
                for e in range(2):
                    store(n_it - 1, e)
                    sp.wait_ge(og_stored[e], 16 * n_it + 16)

            @block.tensor
            def _(pe):
                ident = keep["ident"]

                def bank(i, e, s, b):
                    pe.wait_ge(bank_free[e][b], i * STEPS + (s + 1))

                with nc.tensor.Fori(0, n_it) as i:
                    for s in range(STEPS):
                        for e in range(2):
                            if s == 0:
                                pe.wait_ge(loaded[e], i * 80 + 80)
                            elif s <= NLEV:
                                pe.wait_ge(q_level, i * (2 * NLEV) + (2 * (s - 1) + e + 1))
                                if s >= 2:
                                    pe.wait_ge(k_level, i * (2 * NLEV) + (2 * (s - 1) + e + 1))
                            for b in range(4):
                                bank(i, e, s, b)
                                for r in range(4):
                                    c = 4 * b + r
                                    out = ps[e][b][:, r * P:(r + 1) * P]
                                    toks = slice(c * P, (c + 1) * P)
                                    if s < NLEV:
                                        mm = nc.tensor.matmul(out, k[:, e, toks], q[:, e, toks], start=True, stop=True)
                                    elif s == T_:
                                        mm = nc.tensor.transpose(out, k[:, e, toks], ident[:, :])
                                    elif s == DS_:
                                        if c < TB - 1:
                                            mm = nc.tensor.matmul(out, kt[:, e, c, :], val[:, e, c, :], start=True, stop=True)
                                    else:
                                        mm = nc.tensor.matmul(out, sc[:, e, toks], val[:, e, c, :], start=True, stop=(c == 0))
                                        if c > 0:
                                            mm = nc.tensor.matmul(out, q[:, e, toks], state[:, e, c, :], start=False, stop=True)
                                mm.then_inc(mm_ready[e], 1)

            @block.scalar
            def _(act):
                with nc.scalar.Fori(0, n_it) as i:
                    for s in (6, 7, T_, O_):
                        for e in range(2):
                            for b in range(4):
                                act.wait_ge(mm_ready[e], i * MB + (4 * s + b + 1))
                                src = ps[e][b][:, :].rearrange("p (c n) -> p c n", c=4)
                                dst = sc[:, e, b * 512:(b + 1) * 512].rearrange("p (c n) -> p c n", c=4)
                                if s == 6:
                                    nc.scalar.activation(dst[0:32, :, 32:64], src[0:32, :, 32:64], ACT.Copy)
                                    nc.scalar.activation(dst[64:96, :, 96:128], src[64:96, :, 96:128],
                                                         ACT.Copy).then_inc(bank_free[e][b], 1)
                                elif s == 7:
                                    nc.scalar.activation(dst[0:64, :, 64:128], src[0:64, :, 64:128],
                                                         ACT.Copy).then_inc(bank_free[e][b], 1)
                                elif s == T_:
                                    nc.scalar.activation(kt[:, e, 4 * b:4 * b + 4, :], src, ACT.Copy).then_inc(bank_free[e][b], 1)
                                else:
                                    act.wait_ge(red_ready, i * 8 + (4 * e + b + 1))
                                    nc.scalar.activation(sqr[:, b % 2, :], ps[e][b][:, :], ACT.Square).then_inc(sq_ready, 1)

            @block.gpsimd
            def _(pool):
                def start(i, e):
                    pool.wait_ge(loaded[e], i * 80 + 80)

                with nc.gpsimd.Fori(0, n_it) as i:
                    for s in range(NLEV):
                        for e in range(2):
                            if s == 0:
                                start(i, e)
                                nc.gpsimd.sem_inc(k_level, 1)
                                continue
                            j = s - 1
                            if j > 0:
                                pool.wait_ge(k_level, i * (2 * NLEV) + (2 * (s - 1) + e + 1))
                            pool.wait_ge(q_level, i * (2 * NLEV) + (2 * (s - 1) + e + 1))
                            nc.gpsimd.tensor_tensor(tot_at(e, j + 1), tot_at(e, j).rearrange("p (b s) -> p b s", s=2)[:, :, 0],
                                                    tot_at(e, j).rearrange("p (b s) -> p b s", s=2)[:, :, 1], ALU.mult)
                            pool.wait_ge(mm_ready[e], i * MB + 4 * (s + 1))
                            kk = level_views(k, e, j, 0)
                            nc.gpsimd.tensor_tensor(kk, kk, pair_tot(e, j, 1), ALU.mult).then_inc(k_level, 1)

            @block.vector
            def _(dve):
                nc.vector.memset(sc[:, 0, :], 0.0).then_inc(zeroed, 1)
                nc.vector.memset(sc[:, 1, :], 0.0).then_inc(zeroed, 1)
                nc.vector.memset(state[:, :, 0, :], 0.0).then_inc(zeroed, 1)
                for e in range(2):
                    for b in range(4):
                        nc.vector.sem_inc(bank_free[e][b], 1)
                nc.vector.sem_inc(red_ready, 2)
                dve.wait_ge(mask_in, 16)
                dve.wait_ge(zeroed, 3)
                with nc.vector.Fori(0, n_it) as i:
                    for s in range(NLEV):
                        for e in range(2):
                            if s < NPRED:
                                for b in range(4):
                                    dve.wait_ge(mm_ready[e], i * MB + (4 * s + b + 1))
                                    nc.vector.sem_inc(passed, 1)
                                    dst = sc[:, e, b * 512:(b + 1) * 512].rearrange("p (c n) -> p c n", c=4)
                                    nc.vector.copy_predicated(dst, mask[:, s, :].unsqueeze(1).to_broadcast([P, 4, P]),
                                                              ps[e][b][:, :].rearrange("p (c n) -> p c n", c=4)).then_inc(bank_free[e][b], 1)
                            else:
                                dve.wait_ge(mm_ready[e], i * MB + 4 * (s + 1))
                            if s == 0:
                                nc.vector.tensor_tensor(q[:, e, :], q[:, e, :], f[:, e, :], ALU.mult).then_inc(q_level, 1)
                            else:
                                j = s - 1
                                dve.wait_ge(q_level, i * (2 * NLEV) + (2 * (s - 1) + e + 1))
                                dve.wait_ge(k_level, i * (2 * NLEV) + (2 * (s - 1) + e + 1))
                                qq = level_views(q, e, j, 1)
                                nc.vector.tensor_tensor(qq, qq, pair_tot(e, j, 0), ALU.mult).then_inc(q_level, 1)
                    for e in range(2):
                        decay = tot_at(e, 7)
                        dve.wait_ge(k_level, i * (2 * NLEV) + (2 * NLEV - 1 + e))
                        for c in range(TB - 1):
                            b, r = c // 4, c % 4
                            if r == 0:
                                dve.wait_ge(mm_ready[e], i * MB + (4 * DS_ + b + 1))
                            if c > 0:
                                dve.wait_ge(st_step, i * (2 * (TB - 1)) + (e * (TB - 1) + c))
                            nc.vector.scalar_tensor_tensor(state[:, e, c + 1, :], state[:, e, c, :], decay[:, c:c + 1],
                                                           ps[e][b][:, r * P:(r + 1) * P], ALU.mult, ALU.add).then_inc(st_step, 1)
                            if r == 3 or c == TB - 2:
                                dve.wait_ge(st_step, i * (2 * (TB - 1)) + (e * (TB - 1) + c + 1))
                                nc.vector.sem_inc(bank_free[e][b], 1)
                    for e in range(2):
                        dve.wait_ge(og_stored[e], i * 16 + 16)
                        for b in range(4):
                            dve.wait_ge(sq_ready, i * 8 + (4 * e + b + 1))
                            nc.vector.tensor_reduce(keep["stats"][:, bass.ds((i * 2 + e) * TB + 4 * b, 4)],
                                                    sqr[:, b % 2, :].rearrange("p (c n) -> p c n", c=4), AX.X,
                                                    ALU.add).then_inc(red_ready, 1)
                            nc.vector.tensor_tensor(og[:, e, 4 * b:4 * b + 4, :], ps[e][b][:, :].rearrange("p (c n) -> p c n", c=4),
                                                    gat[:, e, 4 * b:4 * b + 4, :], ALU.mult).then_inc(og_ready, 1)
                            dve.wait_ge(og_ready, i * 8 + (4 * e + b + 1))
                            nc.vector.sem_inc(bank_free[e][b], 1)


def stick(nc, io, keep, scr, o_scr):
    units = [(qb, c, P * (qb % 4 + 1) if c == qb // 4 else 512)
             for qb in range(TB) for c in range(qb // 4, -1, -1)]
    NP = len(units)
    PP = 2 * NP
    SCALE = float(SD) ** -0.5
    with ExitStack() as stack:
        m = Mem(nc, stack)
        q = m.sb("aq", [P, 2, SEQ], F32R)
        k_hi = m.sb("ak_hi", [P, 2, SEQ], F32R)
        k_lo = m.sb("ak_lo", [P, 2, SEQ], F32R)
        val = m.sb("av", [P, 2, TB, SD])
        gat = m.sb("ag", [P, 2, TB, SD])
        beta = m.sb("beta", [P, 4, 512])
        left = m.sb("left", [P, 4, 512])
        run = m.sb("run", [P, 2, SEQ + 1])
        w = m.sb("w", [P, 4, 512])
        wt = m.sb("wt", [P, 4, 512])
        og = m.sb("aog", [P, TB, 2, SD])
        sqr = m.sb("asqr", [P, 2, 512])
        z_ps = [m.ps(f"z_ps{i}", [P, 512]) for i in range(2)]
        t_ps = [m.ps(f"t_ps{i}", [P, 512]) for i in range(2)]
        o_ps = [m.ps(f"o_ps{i}", [P, 512]) for i in range(4)]

        loaded = [m.sem(f"a_loaded{e}") for e in range(2)]
        ones_set = m.sem("ones_set")
        passed = m.sem("a_passed")
        z_ready = m.sem("z_ready")
        beta_ready = m.sem("beta_ready")
        mask_ready = m.sem("mask_ready")
        left_ready = m.sem("left_ready")
        run_ready = m.sem("run_ready")
        w_ready = m.sem("w_ready")
        t_ready = m.sem("t_ready")
        wt_ready = m.sem("wt_ready")
        av_ready = m.sem("av_ready")
        sq_ready = m.sem("asq_ready")
        red_ready = m.sem("ared_ready")
        o_free = m.sem("o_free")
        og_stored = m.sem("aog_stored")
        n_it = SH // 2
        LAG_T, LAG_WT, LAG_AV, LAG_SQ, LAG_OUT = 3, 4, 5, 7, 8
        half_end = [max(n for n in range(NP) if units[n][0] // 8 == h) for h in range(2)]

        def at(n):
            e = n // NP % 2
            qb, c, width = units[n % NP]
            return e, qb, c, width

        def half_done(n):
            e = n // NP % 2
            for h in range(2):
                if n % NP == half_end[h]:
                    return e, h
            return None

        def sweep(eng, step):
            for n in range(LAG_OUT):
                step(0, n, False)
            with eng.Fori(0, n_it - 1) as i:
                for n in range(LAG_OUT, PP + LAG_OUT):
                    step(i, n, False)
            for n in range(LAG_OUT, PP + LAG_OUT):
                step(n_it - 1, n, True)

        def there(n, last):
            return 0 <= n and not (last and n >= PP)

        with nc.Block() as block:
            @block.sync
            def _(sp):
                def load(i, e, first):
                    if not first:
                        sp.wait_ge(av_ready, (i - 1) * PP + (NP * (e + 1) + 4))
                        sp.wait_ge(o_free, (i - 1) * 4 + (2 * (e + 1) + 4))
                    hd = i * 2 + e
                    rows = bass.ds(hd * SD, SD)
                    for dst, half, src in ((q, 0, scr["sq"][0]), (q, 1, scr["sq"][1]), (k_hi, 0, scr["sk"][0]),
                                           (k_hi, 1, scr["sk"][0]), (k_lo, 0, scr["sk"][1]), (k_lo, 1, scr["sk"][1])):
                        sp.dma_start(dst[half * SD:(half + 1) * SD, e, :].bitcast(F32), src[rows, :]).then_inc(loaded[e], 16)
                    sp.dma_start(val[:, e], scr["sv"][0][:, :, rows].rearrange("b p n -> p b n")).then_inc(loaded[e], 16)
                    sp.dma_start(gat[:, e], scr["sg"][0][:, :, rows].rearrange("b p n -> p b n")).then_inc(loaded[e], 16)

                def store(i):
                    sp.wait_ge(o_free, i * 4 + 8)
                    cols = bass.ds(i * (2 * SD) + D, 2 * SD)
                    sp.dma_start(o_scr[:, :, cols].rearrange("b p n -> p b n"), og[:, :].rearrange("p b e n -> p b (e n)")).then_inc(og_stored, 16)

                sp.sem_inc(og_stored, 16)
                load(0, 0, True)
                load(0, 1, True)
                with nc.sync.Fori(0, n_it - 1) as j:
                    load(j + 1, 0, False)
                    store(j)
                    load(j + 1, 1, False)
                store(n_it - 1)
                sp.wait_ge(og_stored, 16 * n_it + 16)

            @block.tensor
            def _(pe):
                nc.tensor.sem_inc(t_ready, 4)
                nc.tensor.sem_inc(av_ready, 4)
                pe.wait_ge(ones_set, 1)

                def step(i, n, last):
                    if there(n, last):
                        e, qb, c, width = at(n)
                        if n % NP == 0:
                            pe.wait_ge(loaded[e], i * 128 + (128 if n < PP else 256))
                        pe.wait_ge(beta_ready, i * PP + (n + 1))
                        for j, kk in enumerate((k_hi, k_lo)):
                            mm = nc.tensor.matmul(z_ps[n % 2][:, 0:width], q[:, e, qb * P:(qb + 1) * P],
                                                  kk[:, e, c * 512:c * 512 + width], start=(j == 0), stop=(j == 1))
                        mm.then_inc(z_ready, 1)
                    n1 = n - LAG_T
                    if there(n1, last):
                        e, qb, c, width = at(n1)
                        pe.wait_ge(w_ready, i * PP + (n1 + 1 + 4))
                        pe.wait_ge(wt_ready, i * PP + (n1 + 1))
                        for j in range(width // P):
                            mm = nc.tensor.transpose(t_ps[n1 % 2][:, j * P:(j + 1) * P], w[:, n1 % 4, j * P:(j + 1) * P], keep["ident"][:, :])
                        mm.then_inc(t_ready, 1)
                    n2 = n - LAG_AV
                    if there(n2, last):
                        e, qb, c, width = at(n2)
                        pe.wait_ge(wt_ready, i * PP + (n2 + 1 + 2))
                        if c == qb // 4 and qb % 8 == 0:
                            pe.wait_ge(o_free, i * 4 + (2 * e + qb // 8 + 1 + (4 if n2 >= PP else 0)))
                        out = o_ps[2 * e + qb // 8][:, (qb % 8) * SD:(qb % 8 + 1) * SD]
                        for j in range(width // P):
                            mm = nc.tensor.matmul(out, wt[:, n2 % 4, j * P:(j + 1) * P], val[:, e, 4 * c + j, :],
                                                  start=(c == qb // 4 and j == 0), stop=(c == 0 and j == width // P - 1))
                        mm.then_inc(av_ready, 1)

                sweep(nc.tensor, step)

            @block.scalar
            def _(act):
                nc.scalar.sem_inc(beta_ready, 2)
                nc.scalar.sem_inc(wt_ready, 2)

                def step(i, n, last):
                    if there(n, last):
                        width = at(n)[3]
                        act.wait_ge(z_ready, i * PP + (n + 1))
                        act.wait_ge(w_ready, i * PP + (n + 1))
                        nc.scalar.activation(beta[:, n % 4, 0:width], z_ps[n % 2][:, 0:width], ACT.Sigmoid,
                                             scale=SCALE).then_inc(beta_ready, 1)
                    n1 = n - LAG_WT
                    if there(n1, last):
                        width = at(n1)[3]
                        act.wait_ge(t_ready, i * PP + (n1 + 1 + 4))
                        act.wait_ge(av_ready, i * PP + (n1 + 1))
                        nc.scalar.activation(wt[:, n1 % 4, 0:width], t_ps[n1 % 2][:, 0:width], ACT.Copy).then_inc(wt_ready, 1)
                    n2 = n - LAG_SQ
                    if there(n2, last) and half_done(n2):
                        e, h = half_done(n2)
                        act.wait_ge(av_ready, i * PP + (n2 + 1 + 4))
                        act.wait_ge(red_ready, i * 4 + (2 * e + h + 1 + (4 if n2 >= PP else 0)))
                        nc.scalar.activation(sqr[:, h, :], o_ps[2 * e + h][:, :], ACT.Square).then_inc(sq_ready, 1)

                sweep(nc.scalar, step)

            @block.gpsimd
            def _(pool):
                def step(i, n, last):
                    if there(n, last):
                        e, qb, c, width = at(n)
                        pool.wait_ge(beta_ready, i * PP + (n + 1 + 2))
                        if c == qb // 4:
                            diag = beta[:, n % 4, width - P:width]
                            nc.gpsimd.sem_inc(passed, 1)
                            nc.gpsimd.affine_select(out=diag, in_=diag, compare_op=ALU.is_gt, fill=0.0, base=0,
                                                    pattern=[[-1, P]], channel_multiplier=1).then_inc(mask_ready, 1)
                            pool.wait_ge(mask_ready, i * (2 * TB) + ((n // NP) * TB + qb + 1))
                        nc.gpsimd.sem_inc(passed, 1)
                        nc.gpsimd.tensor_scalar(left[:, n % 4, 0:width], beta[:, n % 4, 0:width], -1.0, 1.0,
                                                ALU.mult, ALU.add).then_inc(left_ready, 1)

                sweep(nc.gpsimd, step)

            @block.vector
            def _(dve):
                nc.vector.sem_inc(w_ready, 4)
                nc.vector.sem_inc(red_ready, 2)
                nc.vector.sem_inc(o_free, 4)
                nc.vector.memset(run[:, :, SEQ:SEQ + 1], 1.0).then_inc(ones_set, 1)
                dve.wait_ge(ones_set, 1)

                def step(i, n, last):
                    if there(n, last):
                        e, qb, c, width = at(n)
                        lo = SEQ - (qb + 1) * P + c * 512
                        u = qb % 2
                        dve.wait_ge(left_ready, i * PP + (n + 1))
                        if n > 0:
                            dve.wait_ge(run_ready, i * PP + n)
                        if c == qb // 4:
                            dve.wait_ge(w_ready, i * PP + (n + 3))
                        back = run[:, u, lo:lo + width][:, ::-1]
                        nc.vector.tensor_tensor_scan(back, left[:, n % 4, 0:width][:, ::-1], left[:, n % 4, 0:width],
                                                     run[:, u, lo + width:lo + width + 1], ALU.mult, ALU.bypass).then_inc(run_ready, 1)
                    n1 = n - 1
                    if there(n1, last):
                        e, qb, c, width = at(n1)
                        lo = SEQ - (qb + 1) * P + c * 512
                        dve.wait_ge(run_ready, i * PP + (n1 + 1))
                        dve.wait_ge(t_ready, i * PP + (n1 + 1))
                        nc.vector.tensor_tensor(w[:, n1 % 4, 0:width], beta[:, n1 % 4, 0:width],
                                                run[:, qb % 2, lo + 1:lo + width + 1], ALU.mult).then_inc(w_ready, 1)
                    n2 = n - LAG_OUT
                    if there(n2, last) and half_done(n2):
                        e, h = half_done(n2)
                        nxt = 1 if n2 >= PP else 0
                        dve.wait_ge(sq_ready, i * 4 + (2 * e + h + 1 + 4 * nxt))
                        nc.vector.tensor_reduce(keep["stats"][:, bass.ds(i * (2 * TB) + ((GH + e + 2 * nxt) * TB + 8 * h), 8)],
                                                sqr[:, h, :].rearrange("p (b n) -> p b n", n=SD), AX.X, ALU.add).then_inc(red_ready, 1)
                        dve.wait_ge(og_stored, i * 16 + 16 * nxt + 16)
                        nc.vector.tensor_tensor(og[:, 8 * h:8 * h + 8, e, :], o_ps[2 * e + h][:, :].rearrange("p (b n) -> p b n", n=SD),
                                                gat[:, e, 8 * h:8 * h + 8, :], ALU.mult).then_inc(o_free, 1)

                sweep(nc.vector, step)


def output(nc, io, keep, o_scr, out):
    with ExitStack() as stack:
        m = Mem(nc, stack)
        w_raw = m.sb("wo_raw", [P, 2, D])
        w_hi = m.sb("wo_hi", [P, KO, D], F32R)
        w_lo = m.sb("wo_lo", [P, KO, D], F32R)
        o = m.sb("o", [P, 2, 2 * D])
        ot_hi = m.sb("ot_hi", [P, 2, 4, 512], F32R)
        ot_lo = m.sb("ot_lo", [P, 2, 4, 512], F32R)
        x = m.sb("ox", [P, 2, D])
        g_out = m.sb("g_out", [P, D])
        rv = m.sb("rv", [P, 3, NHEAD * TB])
        fin = m.sb("fin", [P, 5])
        t_ps = [m.ps(f"ot_ps{i}", [P, 512]) for i in range(4)]
        y_ps = [m.ps(f"y_ps{i}", [P, D]) for i in range(2)]

        w_loaded = [m.sem(f"wo_loaded{i}") for i in range(2)]
        w_split = m.sem("wo_split")
        g_in = m.sem("g_in")
        o_in = [m.sem(f"o_in{i}") for i in range(2)]
        root_in = m.sem("root_in")
        root_ready = m.sem("oroot_ready")
        r_step = m.sem("r_step")
        on_ready = m.sem("on_ready")
        t_ready = m.sem("ot_ready")
        hi_ready = m.sem("ohi_ready")
        lo_ready = m.sem("olo_ready")
        y_ready = m.sem("y_ready")
        y_step = m.sem("y_step")
        y_taken = m.sem("y_taken")
        sum_ready = m.sem("sum_ready")
        var_ready = m.sem("ovar_ready")
        froot_ready = m.sem("froot_ready")
        out_ready = m.sem("out_ready")
        out_stored = [m.sem(f"out_stored{i}") for i in range(2)]
        n_it = TB // 2
        YS = 8

        with nc.Block() as block:
            @block.sync
            def _(sp):
                sp.sem_inc(out_stored[0], 16)
                sp.sem_inc(out_stored[1], 16)

                def load(tb, e):
                    sp.dma_start(o[:, e, :], o_scr[bass.ds(tb, 1)].rearrange("a p n -> p (a n)")).then_inc(o_in[e], 16)
                    sp.dma_start(x[:, e, :], io["x_blocks"][bass.ds(tb, 1)].rearrange("a p n -> p (a n)")).then_inc(o_in[e], 16)

                load(0, 0)
                load(1, 1)
                sp.dma_start(g_out[:, :], io["final_g"].partition_broadcast(P)).then_inc(g_in, 16)
                for k in range(KO):
                    if k >= 2:
                        sp.wait_ge(w_split, 2 * (k - 1))
                    sp.dma_start(w_raw[:, k % 2, :], io["w_out"][:, k, :]).then_inc(w_loaded[k % 2], 16)

                def store(i, e):
                    sp.wait_ge(out_ready, i * 2 + (e + 1))
                    sp.dma_start(out[bass.ds(i * 2 + e, 1)].rearrange("a p n -> p (a n)"), x[:, e, :]).then_inc(out_stored[e], 16)
                    sp.wait_ge(out_stored[e], i * 16 + 32)

                with nc.sync.Fori(0, n_it - 1) as i:
                    for e in range(2):
                        store(i, e)
                        load(i * 2 + (e + 2), e)
                for e in range(2):
                    store(n_it - 1, e)

            @block.gpsimd
            def _(pool):
                for k in range(KO):
                    pool.wait_ge(w_loaded[k % 2], 16 * (k // 2 + 1))
                    nc.gpsimd.tensor_copy(w_hi[:, k, :], w_raw[:, k % 2, :]).then_inc(w_split, 1)
                    pool.wait_ge(w_split, 2 * k + 1)
                    nc.gpsimd.tensor_tensor(w_lo[:, k, :], w_raw[:, k % 2, :], w_hi[:, k, :].bitcast(F32),
                                            ALU.subtract).then_inc(w_split, 1)

            @block.tensor
            def _(pe):
                nc.tensor.sem_inc(y_ready, 2)

                def transposes(i, e):
                    pe.wait_ge(on_ready, i * 4 + 2 * (e + 1))
                    for b in range(4):
                        pe.wait_ge(lo_ready, i * 8 + (4 * e + b + 1))
                        for r in range(4):
                            j = 4 * b + r
                            mm = nc.tensor.transpose(t_ps[b][:, r * P:(r + 1) * P], o[:, e, j * P:(j + 1) * P], keep["ident"][:, :])
                        mm.then_inc(t_ready, 1)

                def products(i, e):
                    pe.wait_ge(lo_ready, i * 8 + (4 * e + 4 + 4))
                    pe.wait_ge(y_taken, i * 2 + (e + 1))
                    for h in range(2):
                        n = 0
                        for ot, wt in ((ot_hi, w_hi), (ot_lo, w_hi), (ot_hi, w_lo)):
                            for k in range(KO):
                                mm = nc.tensor.matmul(y_ps[e][:, h * 512:(h + 1) * 512], ot[:, e, k // 4, (k % 4) * P:(k % 4 + 1) * P],
                                                      wt[:, k, h * 512:(h + 1) * 512], start=(n == 0), stop=(n == 3 * KO - 1))
                                n += 1
                    mm.then_inc(y_ready, 1)

                transposes(0, 0)
                pe.wait_ge(w_split, 2 * KO)
                with nc.tensor.Fori(0, n_it - 1) as i:
                    transposes(i, 1)
                    products(i, 0)
                    transposes(i + 1, 0)
                    products(i, 1)
                transposes(n_it - 1, 1)
                products(n_it - 1, 0)
                products(n_it - 1, 1)

            @block.scalar
            def _(act):
                act.wait_ge(root_in, 1)
                nc.scalar.activation(rv[:, 1, :], rv[:, 0, :], ACT.Sqrt).then_inc(root_ready, 1)

                def split(i, e):
                    for b in range(4):
                        act.wait_ge(t_ready, i * 8 + (4 * e + b + 1))
                        act.wait_ge(y_ready, i * 2 + (e + 1))
                        nc.scalar.activation(ot_hi[:, e, b, :], t_ps[b][:, :], ACT.Copy).then_inc(hi_ready, 1)

                def final(i, e):
                    act.wait_ge(y_step, i * (2 * YS) + (e * YS + 3))
                    nc.scalar.activation(o[:, e, 0:D], x[:, e, :], ACT.Square, accum_out=fin[:, 0:1]).then_inc(sum_ready, 1)
                    act.wait_ge(var_ready, i * 2 + (e + 1))
                    nc.scalar.activation(fin[:, 2:3], fin[:, 1:2], ACT.Sqrt).then_inc(froot_ready, 1)

                split(0, 0)
                with nc.scalar.Fori(0, n_it - 1) as i:
                    split(i, 1)
                    final(i, 0)
                    split(i + 1, 0)
                    final(i, 1)
                split(n_it - 1, 1)
                final(n_it - 1, 0)
                final(n_it - 1, 1)

            @block.vector
            def _(dve):
                nc.vector.sem_inc(lo_ready, 4)
                nc.vector.sem_inc(y_taken, 2)
                n_g = GH * TB
                n_all = NHEAD * TB
                var, root, a = (rv[:, j, :] for j in range(3))
                stats = keep["stats"]
                r = keep["stats"][:, :]
                nc.vector.tensor_scalar(rv[:, 0, 0:n_g], stats[:, 0:n_g], 1.0 / GD, EPS, ALU.mult, ALU.add).then_inc(r_step, 1)
                nc.vector.tensor_scalar(rv[:, 0, n_g:n_all], stats[:, n_g:n_all], 1.0 / SD, EPS, ALU.mult, ALU.add).then_inc(root_in, 1)
                dve.wait_ge(r_step, 1)
                dve.wait_ge(root_ready, 1)
                nc.vector.reciprocal(r, root).then_inc(r_step, 1)
                dve.wait_ge(r_step, 2)
                nc.vector.tensor_tensor(a, r, r, ALU.mult).then_inc(r_step, 1)
                dve.wait_ge(r_step, 3)
                nc.vector.tensor_tensor(a, a, var, ALU.mult).then_inc(r_step, 1)
                dve.wait_ge(r_step, 4)
                nc.vector.tensor_scalar(a, a, -0.5, 1.5, ALU.mult, ALU.add).then_inc(r_step, 1)
                dve.wait_ge(r_step, 5)
                nc.vector.tensor_tensor(r, r, a, ALU.mult).then_inc(r_step, 1)
                dve.wait_ge(r_step, 6)
                dve.wait_ge(g_in, 16)

                def head_norm(i, e):
                    dve.wait_ge(o_in[e], i * 32 + 32)
                    rr = r.rearrange("p (h t) -> p h t", t=TB)[:, :, bass.ds(i * 2 + e, 1)]
                    for lo, h0, nh, dh in ((0, 0, GH, GD), (D, GH, SH, SD)):
                        v = o[:, e, lo:lo + D].rearrange("p (h n) -> p h n", n=dh)
                        nc.vector.tensor_tensor(v, v, rr[:, h0:h0 + nh, :].to_broadcast([P, nh, dh]), ALU.mult).then_inc(on_ready, 1)

                def split(i, e):
                    for b in range(4):
                        dve.wait_ge(hi_ready, i * 8 + (4 * e + b + 1))
                        nc.vector.tensor_tensor(ot_lo[:, e, b, :], t_ps[b][:, :], ot_hi[:, e, b, :].bitcast(F32),
                                                ALU.subtract).then_inc(lo_ready, 1)

                def final(i, e):
                    at = [i * (2 * YS) + e * YS, 0]

                    def done(ins):
                        at[1] += 1
                        ins.then_inc(y_step, 1)
                        dve.wait_ge(y_step, at[0] + at[1])

                    dve.wait_ge(y_ready, i * 2 + (e + 3))
                    done(nc.vector.tensor_tensor(o[:, e, 0:512], y_ps[e][:, 0:512], keep["gate"][:, 0:512], ALU.mult))
                    nc.vector.tensor_tensor(o[:, e, 512:D], y_ps[e][:, 512:D], keep["gate"][:, 512:D], ALU.mult).then_inc(y_taken, 1)
                    dve.wait_ge(y_taken, i * 2 + (e + 3))
                    done(nc.vector.tensor_tensor(x[:, e, 0:512], x[:, e, 0:512], o[:, e, 0:512], ALU.add))
                    done(nc.vector.tensor_tensor(x[:, e, 512:D], x[:, e, 512:D], o[:, e, 512:D], ALU.add))
                    dve.wait_ge(sum_ready, i * 2 + (e + 1))
                    nc.vector.tensor_scalar(fin[:, 1:2], fin[:, 0:1], 1.0 / D, EPS, ALU.mult, ALU.add).then_inc(var_ready, 1)
                    dve.wait_ge(froot_ready, i * 2 + (e + 1))
                    done(nc.vector.reciprocal(fin[:, 3:4], fin[:, 2:3]))
                    done(nc.vector.tensor_tensor(fin[:, 4:5], fin[:, 3:4], fin[:, 3:4], ALU.mult))
                    done(nc.vector.tensor_tensor(fin[:, 4:5], fin[:, 4:5], fin[:, 1:2], ALU.mult))
                    done(nc.vector.tensor_scalar(fin[:, 4:5], fin[:, 4:5], -0.5, 1.5, ALU.mult, ALU.add))
                    done(nc.vector.tensor_tensor(fin[:, 3:4], fin[:, 3:4], fin[:, 4:5], ALU.mult))
                    nc.vector.scalar_tensor_tensor(x[:, e, :], x[:, e, :], fin[:, 3:4], g_out[:, :],
                                                   ALU.mult, ALU.mult).then_inc(out_ready, 1)

                head_norm(0, 0)
                split(0, 0)
                head_norm(0, 1)
                with nc.vector.Fori(0, n_it - 1) as i:
                    split(i, 1)
                    final(i, 0)
                    head_norm(i + 1, 0)
                    split(i + 1, 0)
                    final(i, 1)
                    head_norm(i + 1, 1)
                split(n_it - 1, 1)
                final(n_it - 1, 0)
                final(n_it - 1, 1)


def build(nc, io, out):
    scr = {
        "gq": [nc.dram_tensor("s_gq", (D, SEQ), F32).ap()],
        "gf": [nc.dram_tensor(f"s_g{n}", (D, SEQ), F32).ap() for n in "fk"],
        "sq": [nc.dram_tensor(f"s_q{n}", (D, SEQ), F32).ap() for n in ("hi", "lo")],
        "sk": [nc.dram_tensor(f"s_k{n}", (D, SEQ), F32).ap() for n in ("hi", "lo")],
    }
    for name in ("gi", "gg", "sv", "sg"):
        scr[name] = [nc.dram_tensor(f"s_{name}", (TB, P, D), F32).ap()]
    o_scr = nc.dram_tensor("s_o", (TB, P, 2 * D), F32).ap()
    with ExitStack() as stack:
        m = Mem(nc, stack)
        keep = {
            "ident": m.sb("ident", [P, P]),
            "gate": m.sb("gate", [P, D]),
            "lb": m.sb("lb", [P, 2, GH]),
            "g_hgrn": m.sb("g_hgrn", [P, GD]),
            "g_stick": m.sb("g_stick", [P, SD]),
            "stats": m.sb("stats", [P, NHEAD * TB]),
        }
        with ExitStack() as hstack:
            hm = Mem(nc, hstack)
            h_hi = hm.sb("h_hi", [P, KD, SEQ], F32R)
            h_lo = hm.sb("h_lo", [P, KD, SEQ], F32R)
            condition(nc, io, keep, h_hi, h_lo)
            project(nc, io, keep, h_hi, h_lo, scr)
        hgrn(nc, io, keep, scr, o_scr)
        stick(nc, io, keep, scr, o_scr)
        output(nc, io, keep, o_scr, out)


def level_masks(np):
    s, t = np.arange(P)[:, None], np.arange(P)[None, :]
    masks = [s == t]
    for j in range(NPRED - 1):
        b = 1 << j
        masks.append((t // b == s // b + 1) & (s // b % 2 == 0))
    return np.stack(masks, 1).astype(np.int32)


def kernel(x, c, w_ada, b_ada, norm_g, w_in, lb_logits, hgrn_norm_g, sb_norm_g, w_out, final_g):
    import numpy as np
    import concourse.bacc as bacc
    from concourse.bass_utils import run_bass_kernel_spmd

    def col(v):
        return np.asarray(v).reshape(KD, P).T

    x = np.asarray(x)[0]
    b_ada = np.asarray(b_ada)[0]
    w_in = np.asarray(w_in)[0].reshape(KD, P, 8, CH_T, WC)
    w_in = w_in[:, :, [p[2] for p in PROJ]]
    arrays = {
        "x": x,
        "small": np.stack([col(c), col(b_ada[:D]), col(b_ada[D:2 * D]), col(norm_g), col(lb_logits)], 1),
        "b_gate": b_ada[2 * D:],
        "w_ada": np.asarray(w_ada)[0].reshape(KD, P, 12, 256).transpose(2, 1, 0, 3),
        "w_in": w_in.transpose(2, 3, 1, 0, 4).reshape(NCH, P, KD, WC),
        "w_out": np.asarray(w_out)[0].reshape(KO, P, D).transpose(1, 0, 2),
        "g_hgrn": np.asarray(hgrn_norm_g)[0],
        "g_stick": np.asarray(sb_norm_g)[0],
        "final_g": np.asarray(final_g),
        "ident": np.eye(P, dtype=np.float32),
        "mask": level_masks(np),
    }
    nc = bacc.Bacc("TRN2", target_bir_lowering=False, num_devices=1)
    io, ins = {}, {}
    for name, a in arrays.items():
        a = np.ascontiguousarray(a)
        ins[f"in_{name}"] = a
        io[name] = nc.dram_tensor(f"in_{name}", a.shape, mybir.dt.from_np(a.dtype), kind="ExternalInput").ap()
    io["x_blocks"] = io["x"].rearrange("(b p) n -> b p n", p=P)
    out = nc.dram_tensor("out", (TB, P, D), F32, kind="ExternalOutput").ap()
    build(nc, io, out)
    r = run_bass_kernel_spmd(nc, [ins], core_ids=[0])
    return r.results[0]["out"].reshape(1, SEQ, D)
```

```python
from contextlib import ExitStack

import concourse.bass as bass
from concourse import mybir

F32 = mybir.dt.float32
F32R = mybir.dt.float32r
I32 = mybir.dt.int32
BF16 = mybir.dt.bfloat16
ALU = mybir.AluOpType
ACT = mybir.ActivationFunctionType
AX = mybir.AxisListType

P = 128
D = 1024
SEQ = 2048
KD = D // P
TB = SEQ // P
TG = SEQ // 512
EPS = 1e-6
GH = 8
GD = 128
SH = 16
SD = 64
NHEAD = GH + SH
WC = 256
NCH = 8 * D // WC
CH_T = D // WC
KO = 2 * D // P
NLEV = 8
NPRED = 6


class Mem:

    def __init__(self, nc, stack):
        self.nc, self.stack = nc, stack

    def sb(self, name, shape, dt=F32):
        return self.stack.enter_context(self.nc.sbuf_tensor(name, shape, dt))

    def ps(self, name, shape):
        return self.stack.enter_context(self.nc.psum_tensor(name, shape, F32))

    def sem(self, name):
        return self.stack.enter_context(self.nc.semaphore(name))


def condition(nc, io, keep, h_hi, h_lo, w_raw, w_first):
    with ExitStack() as stack:
        m = Mem(nc, stack)
        AC = 256
        n_ada = 3 * D // AC
        n_mod = 2 * D // AC
        slots = [n % 3 if n < n_mod + 1 else n % 2 for n in range(n_ada)]

        def slot(n):
            return ada[:, slots[n]] if slots[n] < 2 else w_raw[:, :, :]

        def earlier(n):
            return [j for j in range(n) if slots[j] == slots[n]]

        ada = m.sb("ada", [P, 2, KD, AC])
        xg = m.sb("xg", [P, 2, 4, D])
        c_act = m.sb("c_act", [P, KD, P])
        small = m.sb("small", [P, 5, KD])
        c_sig = m.sb("c_sig", [P, KD])
        c_col = m.sb("c_col", [P, KD])
        diag = m.sb("diag", [P, 2, P])
        mod_col = m.sb("mod_col", [P, 2, KD])
        shift = m.sb("shift", [P, KD])
        mul = m.sb("mul", [P, KD])
        lb_tmp = m.sb("lb_tmp", [P, 3, GH])
        stat = m.sb("stat", [P, 5, 4])
        hx = m.sb("hx", [P, 2, 512])
        mod_ps = [m.ps(f"mod_ps{i}", [P, 512]) for i in range(2)]
        xt_ps = [m.ps(f"xt_ps{i}", [P, 512]) for i in range(4)]
        junk = m.ps("junk", [P, D])

        ada_in = [m.sem(f"ada_in{i}") for i in range(3)]
        x_in = [m.sem(f"x_in{i}") for i in range(2)]
        small_in = m.sem("small_in")
        wide_in = m.sem("wide_in")
        act_small = m.sem("act_small")
        cb_ready = m.sem("cb_ready")
        mod_ready = m.sem("mod_ready")
        mod_taken = m.sem("mod_taken")
        sq_ready = m.sem("sq_ready")
        var_ready = m.sem("var_ready")
        root_ready = m.sem("root_ready")
        xn_ready = m.sem("xn_ready")
        xt_ready = m.sem("xt_ready")
        col_ready = m.sem("col_ready")
        hi_ready = m.sem("hi_ready")
        hx_ready = m.sem("hx_ready")
        lo_ready = m.sem("lo_ready")
        dve_step = m.sem("dve_step")

        with nc.Block() as block:
            @block.sync
            def _(sp):
                def load_ada(n):
                    if earlier(n):
                        sp.wait_ge(mod_ready, earlier(n)[-1] + 1)
                    sp.dma_start(slot(n), io["w_ada"][n]).then_inc(ada_in[slots[n]], 16)

                def load_x(g):
                    if g >= 2:
                        sp.wait_ge(xt_ready, KD * (g - 1))
                    src = io["x"][g * 512:(g + 1) * 512, :].rearrange("(b p) n -> p b n", p=P)
                    sp.dma_start(xg[:, g % 2], src).then_inc(x_in[g % 2], 16)

                sp.dma_start(small[:, :, :], io["small"]).then_inc(small_in, 16)
                sp.dma_start(keep["ident"][:, :], io["ident"]).then_inc(small_in, 16)
                for n in range(3):
                    load_ada(n)
                load_x(0)
                for n in range(3, 6):
                    load_ada(n)
                load_x(1)
                for n in range(6, n_mod + 2):
                    load_ada(n)
                load_x(2)
                load_ada(n_mod + 2)
                load_ada(n_mod + 3)
                load_x(3)
                sp.wait_ge(mod_ready, [n for n in range(n_ada) if slots[n] == 2][-1] + 1)
                sp.dma_start(w_raw[:, :, :], io["w_in"][0]).then_inc(w_first, 16)

            @block.tensor
            def _(pe):
                def modulation(n):
                    pe.wait_ge(ada_in[slots[n]], 16 * (len(earlier(n)) + 1))
                    if n >= 2:
                        pe.wait_ge(mod_taken, n - 1)
                    for k in range(KD):
                        mm = nc.tensor.matmul(mod_ps[n % 2][:, 0:AC], c_act[:, k, :], slot(n)[:, k, :],
                                              start=(k == 0), stop=(k == KD - 1))
                    mm.then_inc(mod_ready, 1)

                pe.wait_ge(cb_ready, 1)
                for n in range(n_mod):
                    modulation(n)
                for g in range(TG):
                    pe.wait_ge(xn_ready, 4 * (g + 1))
                    for k in range(KD):
                        n = g * KD + k
                        if n >= 4:
                            pe.wait_ge(hx_ready, n - 3)
                        for b in range(4):
                            mm = nc.tensor.transpose(xt_ps[n % 4][:, b * P:(b + 1) * P],
                                                     xg[:, g % 2, b, k * P:(k + 1) * P], keep["ident"][:, :])
                        mm.then_inc(xt_ready, 1)
                    modulation(n_mod + g)

            @block.scalar
            def _(act):
                act.wait_ge(small_in, 32)
                nc.scalar.activation(c_sig[:, :], small[:, 0, :], ACT.Sigmoid).then_inc(act_small, 1)
                act.wait_ge(dve_step, 1)
                nc.scalar.activation(lb_tmp[:, 1, :], lb_tmp[:, 0, :], ACT.Exp).then_inc(act_small, 1)
                act.dma_start(keep["gate"][:, :], io["b_gate"].partition_broadcast(P)).then_inc(wide_in, 16)
                act.dma_start(keep["g_hgrn"][:, :], io["g_hgrn"].partition_broadcast(P)).then_inc(wide_in, 16)
                act.dma_start(keep["g_stick"][:, :], io["g_stick"].partition_broadcast(P)).then_inc(wide_in, 16)

                def squares(g):
                    act.wait_ge(x_in[g % 2], 16 * (g // 2 + 1))
                    if g >= 1:
                        act.wait_ge(var_ready, g)
                    for b in range(4):
                        if g or b:
                            act.wait_ge(sq_ready, 4 * g + b)
                        nc.scalar.activation(junk[:, :], xg[:, g % 2, b, :], ACT.Square,
                                             accum_out=stat[:, 0, b:b + 1]).then_inc(sq_ready, 1)
                    act.wait_ge(var_ready, g + 1)
                    nc.scalar.activation(stat[:, 2, :], stat[:, 1, :], ACT.Sqrt).then_inc(root_ready, 1)

                def high(g):
                    for k in range(KD):
                        n = g * KD + k
                        act.wait_ge(xt_ready, n + 1)
                        nc.scalar.activation(h_hi[:, k, g * 512:(g + 1) * 512], xt_ps[n % 4][:, :], ACT.Identity,
                                             bias=shift[:, k:k + 1], scale=mul[:, k:k + 1]).then_inc(hi_ready, 1)

                squares(0)
                squares(1)
                act.wait_ge(col_ready, 1)
                for g in range(TG):
                    high(g)
                    if 1 <= g < TG - 1:
                        squares(g + 1)

            @block.vector
            def _(dve):
                done = [0]

                def step(ins):
                    done[0] += 1
                    ins.then_inc(dve_step, 1)
                    dve.wait_ge(dve_step, done[0])

                dve.wait_ge(small_in, 32)
                step(nc.vector.tensor_tensor(lb_tmp[:, 0, :], small[:, 4, :], small[:, 4, :], ALU.subtract))
                dve.wait_ge(act_small, 1)
                step(nc.vector.tensor_tensor(c_col[:, :], small[:, 0, :], c_sig[:, :], ALU.mult))
                nc.vector.tensor_copy(c_act[:, :, :], c_col[:, :].unsqueeze(2).to_broadcast([P, KD, P])).then_inc(cb_ready, 1)
                dve.wait_ge(act_small, 2)
                step(nc.vector.reciprocal(lb_tmp[:, 2, :], lb_tmp[:, 1, :]))
                step(nc.vector.tensor_tensor(lb_tmp[:, 2, :], lb_tmp[:, 2, :], lb_tmp[:, 1, :], ALU.mult))
                step(nc.vector.tensor_tensor(keep["lb"][:, 0, :], lb_tmp[:, 2, :], lb_tmp[:, 2, :], ALU.subtract))
                step(nc.vector.tensor_scalar(keep["lb"][:, 1, :], keep["lb"][:, 0, :], -1.0, 1.0, ALU.mult, ALU.add))

                def norm(g):
                    dve.wait_ge(sq_ready, 4 * (g + 1))
                    v, root, y, a = (stat[:, j, :] for j in (1, 2, 3, 4))
                    nc.vector.tensor_scalar(v, stat[:, 0, :], 1.0 / D, EPS, ALU.mult, ALU.add).then_inc(var_ready, 1)
                    dve.wait_ge(root_ready, g + 1)
                    step(nc.vector.reciprocal(y, root))
                    step(nc.vector.tensor_tensor(a, y, y, ALU.mult))
                    step(nc.vector.tensor_tensor(a, a, v, ALU.mult))
                    step(nc.vector.tensor_scalar(a, a, -0.5, 1.5, ALU.mult, ALU.add))
                    step(nc.vector.tensor_tensor(y, y, a, ALU.mult))
                    for b in range(4):
                        nc.vector.tensor_scalar(xg[:, g % 2, b, :], xg[:, g % 2, b, :], stat[:, 3, b:b + 1], None,
                                                ALU.mult).then_inc(xn_ready, 1)

                def take_mod(n):
                    dve.wait_ge(mod_ready, n + 1)
                    if n < n_mod:
                        step(nc.vector.tensor_tensor(diag[:, :, :], mod_ps[n % 2][:, 0:AC].rearrange("p (a n) -> p a n", a=2),
                                                     keep["ident"][:, :].unsqueeze(1).to_broadcast([P, 2, P]), ALU.mult))
                        nc.vector.sem_inc(mod_taken, 1)
                        j, a = n // CH_T, 2 * (n % CH_T)
                        step(nc.vector.tensor_reduce(mod_col[:, j, a:a + 2], diag[:, :, :], AX.X, ALU.add))
                    else:
                        dst = keep["gate"][:, (n - n_mod) * AC:(n - n_mod + 1) * AC]
                        nc.vector.tensor_tensor(dst, mod_ps[n % 2][:, 0:AC], dst, ALU.add).then_inc(mod_taken, 1)

                for n in range(3):
                    take_mod(n)
                norm(0)
                for n in range(3, 6):
                    take_mod(n)
                norm(1)
                for n in range(6, n_mod):
                    take_mod(n)
                step(nc.vector.tensor_tensor(shift[:, :], mod_col[:, 0, :], small[:, 1, :], ALU.add))
                step(nc.vector.tensor_tensor(mod_col[:, 1, :], mod_col[:, 1, :], small[:, 2, :], ALU.add))
                step(nc.vector.tensor_scalar(mod_col[:, 1, :], mod_col[:, 1, :], 1.0, None, ALU.add))
                nc.vector.tensor_tensor(mul[:, :], mod_col[:, 1, :], small[:, 3, :], ALU.mult).then_inc(col_ready, 1)
                dve.wait_ge(col_ready, 1)
                dve.wait_ge(wide_in, 48)
                for g in range(TG):
                    for k in range(KD):
                        n = g * KD + k
                        dve.wait_ge(hi_ready, n + 1)
                        if n >= 2:
                            dve.wait_ge(lo_ready, n - 1)
                        nc.vector.tensor_scalar(hx[:, n % 2, :], xt_ps[n % 4][:, :], mul[:, k:k + 1], shift[:, k:k + 1],
                                                ALU.mult, ALU.add).then_inc(hx_ready, 1)
                    take_mod(n_mod + g)
                    if 1 <= g < TG - 1:
                        norm(g + 1)

            @block.gpsimd
            def _(pool):
                for n in range(TG * KD):
                    g, k = n // KD, n % KD
                    pool.wait_ge(hx_ready, n + 1)
                    hi = h_hi[:, k, g * 512:(g + 1) * 512].bitcast(F32)
                    nc.gpsimd.tensor_tensor(h_lo[:, k, g * 512:(g + 1) * 512], hx[:, n % 2, :], hi,
                                            ALU.subtract).then_inc(lo_ready, 1)


PROJ = [("gq", True, 0), ("gf", True, 1), ("sq", True, 4), ("sk", True, 5),
        ("gi", False, 2), ("gg", False, 3), ("sv", False, 6), ("sg", False, 7)]


def project(nc, io, keep, h_hi, h_lo, w_raw, w_first, scr):
    with ExitStack() as stack:
        m = Mem(nc, stack)
        w_hi = m.sb("w_hi", [P, 2, KD, WC], F32R)
        w_lo = m.sb("w_lo", [P, 2, KD, WC], F32R)
        st = m.sb("st", [P, 2, 512])
        st2 = m.sb("st2", [P, 2, 512])
        st_hi = m.sb("st_hi", [P, 2, 512], F32R)
        st_lo = m.sb("st_lo", [P, 2, 512], F32R)
        sg = m.sb("sg", [P, 2, 512])
        sg2 = m.sb("sg2", [P, 2, 512])
        u_ps = [m.ps(f"u_ps{i}", [P, 512]) for i in range(8)]

        w_in_sem = m.sem("w_loaded")
        w_high = m.sem("w_high")
        w_split = m.sem("w_split")
        u_ready = m.sem("u_ready")
        u_act = m.sem("u_act")
        u_taken = m.sem("u_taken")
        g_step = m.sem("g_step")
        staged = m.sem("staged")
        stored = [m.sem(f"stored{i}") for i in range(2)]
        passed = m.sem("w_passed")
        n_pair = NCH // 2

        def tiles():
            return [(par, j) for par in range(2) for j in range(8)]

        with nc.Block() as block:
            @block.gpsimd
            def _(pool):
                def chunk(c, par):
                    pool.wait_ge(w_in_sem, 16 * c)
                    pool.wait_ge(u_ready, 8 * c + 8)
                    nc.gpsimd.sem_inc(passed, 1)
                    nc.gpsimd.tensor_copy(w_hi[:, par], w_raw[:, :, :]).then_inc(w_split, 1)
                    pool.wait_ge(w_split, 2 * c + 1)
                    nc.gpsimd.tensor_tensor(w_lo[:, par], w_raw[:, :, :], w_hi[:, par].bitcast(F32),
                                            ALU.subtract).then_inc(w_split, 1)

                chunk(1, 1)
                with nc.gpsimd.Fori(1, n_pair) as i:
                    for par in range(2):
                        chunk(i * 2 + par, par)

            @block.tensor
            def _(pe):
                nc.tensor.sem_inc(u_ready, 16)

                def tile(c, j, par, feature):
                    pe.wait_ge(u_taken, 8 * c + j + 1)
                    if feature:
                        cg, tp = j // 4, j % 4
                        n = 0
                        for wt, ht in ((w_hi, h_hi), (w_hi, h_lo), (w_lo, h_hi)):
                            for k in range(KD):
                                mm = nc.tensor.matmul(u_ps[j][:, :], wt[:, par, k, cg * P:(cg + 1) * P],
                                                      ht[:, k, tp * 512:(tp + 1) * 512], start=(n == 0), stop=(n == 3 * KD - 1))
                                n += 1
                    else:
                        for b in range(2):
                            tb = 2 * j + b
                            n = 0
                            for wt, ht in ((w_hi, h_hi), (w_hi, h_lo), (w_lo, h_hi)):
                                for k in range(KD):
                                    mm = nc.tensor.matmul(u_ps[j][:, b * WC:(b + 1) * WC], ht[:, k, tb * P:(tb + 1) * P],
                                                          wt[:, par, k, :], start=(n == 0), stop=(n == 3 * KD - 1))
                                    n += 1
                    mm.then_inc(u_ready, 1)

                for half, feature in ((0, True), (1, False)):
                    with nc.tensor.Fori(half * n_pair // 2, (half + 1) * n_pair // 2) as i:
                        for par in range(2):
                            c = i * 2 + par
                            pe.wait_ge(w_split, 2 * c + 2)
                            for j in range(8):
                                tile(c, j, par, feature)

            @block.scalar
            def _(act):
                act.wait_ge(w_first, 16)
                for k in range(KD):
                    nc.scalar.activation(w_hi[:, 0, k, :], w_raw[:, k, :], ACT.Copy).then_inc(w_high, 1)
                for t, (name, feature, _) in enumerate(PROJ):
                    with nc.scalar.Fori(t * CH_T // 2, (t + 1) * CH_T // 2) as i:
                        for par, j in tiles():
                            n = i * 16 + (par * 8 + j)
                            s = j % 2
                            act.wait_ge(u_ready, n + 17)
                            act.wait_ge(u_taken, n + 7)
                            if name in ("sq", "sk"):
                                act.wait_ge(stored[s], i * 256 + 32 * (4 * par + j // 2 + 1))
                                nc.scalar.activation(st_hi[:, s, :], u_ps[j][:, :], ACT.Copy).then_inc(u_act, 1)
                            elif name == "gf":
                                nc.scalar.activation(sg2[:, s, :], u_ps[j][:, :], ACT.Sigmoid, scale=-1.0)
                                nc.scalar.activation(sg[:, s, :], u_ps[j][:, :], ACT.Sigmoid).then_inc(u_act, 1)
                            elif name in ("gi", "sv"):
                                nc.scalar.activation(sg[:, s, :], u_ps[j][:, :], ACT.Copy).then_inc(u_act, 1)
                            else:
                                nc.scalar.activation(sg[:, s, :], u_ps[j][:, :], ACT.Sigmoid).then_inc(u_act, 1)

            @block.vector
            def _(dve):
                nc.vector.sem_inc(u_taken, 8)
                for k in range(KD):
                    dve.wait_ge(w_high, k + 1)
                    ins = nc.vector.tensor_tensor(w_lo[:, 0, k, :], w_raw[:, k, :], w_hi[:, 0, k, :].bitcast(F32), ALU.subtract)
                ins.then_inc(w_split, 2)
                for t, (name, feature, _) in enumerate(PROJ):
                    with nc.vector.Fori(t * CH_T // 2, (t + 1) * CH_T // 2) as i:
                        for par, j in tiles():
                            n = i * 16 + (par * 8 + j)
                            s = j % 2
                            dve.wait_ge(u_act, n + 1)
                            dve.wait_ge(stored[s], i * 256 + 32 * (4 * par + j // 2 + 1))
                            if name == "gq":
                                ins = nc.vector.tensor_tensor(st[:, s, :], u_ps[j][:, :], sg[:, s, :], ALU.mult)
                            elif name == "gf":
                                hd = (i - t * CH_T // 2) * 4 + (par * 2 + j // 4)
                                lb0 = keep["lb"][:, 0, bass.ds(hd, 1)]
                                lb1 = keep["lb"][:, 1, bass.ds(hd, 1)]
                                nc.vector.tensor_scalar(st2[:, s, :], sg2[:, s, :], lb1, None, ALU.mult)
                                ins = nc.vector.tensor_scalar(st[:, s, :], sg[:, s, :], lb1, lb0, ALU.mult, ALU.add)
                            elif name in ("sq", "sk"):
                                ins = nc.vector.tensor_tensor(st_lo[:, s, :], u_ps[j][:, :], st_hi[:, s, :].bitcast(F32), ALU.subtract)
                            elif name in ("gi", "sv"):
                                ins = nc.vector.tensor_copy(st[:, s, :], sg[:, s, :])
                            else:
                                g = keep["g_hgrn" if name == "gg" else "g_stick"]
                                w = GD if name == "gg" else SD
                                g_steps = (t // 2 - 2) * 32
                                nc.vector.tensor_tensor(st2[:, s, :], u_ps[j][:, :], sg[:, s, :], ALU.mult).then_inc(g_step, 1)
                                dve.wait_ge(g_step, (i - t * CH_T // 2) * 16 + (par * 8 + j + 1 + g_steps))
                                ins = nc.vector.tensor_tensor(
                                    st[:, s, :].rearrange("p (a n) -> p a n", n=w), st2[:, s, :].rearrange("p (a n) -> p a n", n=w),
                                    g[:, :].unsqueeze(1).to_broadcast([P, 512 // w, w]), ALU.mult)
                            ins.then_inc(u_taken, 1)

            @block.sync
            def _(sp):
                sp.sem_inc(stored[0], 32)
                sp.sem_inc(stored[1], 32)

                def load_w(c):
                    sp.dma_start(w_raw[:, :, :], io["w_in"][bass.ds(c, 1)].rearrange("a p k n -> p (a k) n")).then_inc(w_in_sem, 16)

                for t, (name, feature, _) in enumerate(PROJ):
                    dsts = scr[name]

                    def pair(i2, last):
                        i = i2 + t * CH_T // 2
                        for par, j in tiles():
                            n = i * 16 + (par * 8 + j)
                            s = j % 2
                            if j == 1 and not (last and par == 1):
                                sp.wait_ge(w_split, i * 4 + (2 * par + 2))
                                load_w(i * 2 + (par + 1))
                            sp.wait_ge(u_taken, n + 9)
                            cc = i2 * 2 + par
                            srcs = (st_hi, st_lo) if name in ("sq", "sk") else (st, st2) if name == "gf" else (st,)
                            for q, (src, dst) in enumerate(zip(srcs, dsts)):
                                if src in (st_hi, st_lo):
                                    src = src[:, :, :].bitcast(F32)
                                if feature:
                                    to = dst[bass.ds(cc * WC + (j // 4) * P, P), (j % 4) * 512:(j % 4 + 1) * 512]
                                    frm = src[:, s, :]
                                else:
                                    to = dst[2 * j:2 * j + 2, :, bass.ds(cc * WC, WC)].rearrange("b p n -> p b n")
                                    frm = src[:, s, :].rearrange("p (b n) -> p b n", b=2)
                                sp.dma_start(to, frm).then_inc(stored[s], 32 // len(srcs))

                    if t < len(PROJ) - 1:
                        with nc.sync.Fori(0, CH_T // 2) as i2:
                            pair(i2, False)
                    else:
                        for i2 in range(CH_T // 2):
                            pair(i2, i2 == CH_T // 2 - 1)
                sp.wait_ge(stored[0], n_pair * 256 + 32)
                sp.wait_ge(stored[1], n_pair * 256 + 32)


def hgrn(nc, io, keep, scr, o_scr):
    with ExitStack() as stack:
        m = Mem(nc, stack)
        q = m.sb("hq", [P, 4, SEQ])
        k = m.sb("hk", [P, 2, SEQ])
        f = m.sb("hf", [P, 2, SEQ])
        val = m.sb("hi", [P, 2, TB, GD])
        gat = m.sb("hg", [P, 2, TB, GD])
        sc = m.sb("hsc", [P, 2, SEQ])
        kt = m.sb("hkt", [P, 2, TB, GD])
        state = m.sb("hst", [P, 2, TB, GD])
        tot = m.sb("htot", [P, 2, SEQ])
        og = m.sb("hog", [P, 2, TB, GD])
        sqr = m.sb("hsqr", [P, 2, 512])
        mask = m.sb("hmask", [P, NPRED, P], I32)
        ps = [[m.ps(f"hps{e}{b}", [P, 512]) for b in range(4)] for e in range(2)]

        mask_in = m.sem("mask_in")
        q_in = [m.sem(f"q_in{s}") for s in range(4)]
        k_in = [m.sem(f"k_in{e}") for e in range(2)]
        f_in = [m.sem(f"f_in{e}") for e in range(2)]
        val_in = [m.sem(f"val_in{e}") for e in range(2)]
        gat_in = [m.sem(f"gat_in{e}") for e in range(2)]
        zeroed = m.sem("h_zeroed")
        mm_ready = [m.sem(f"mm_ready{e}") for e in range(2)]
        bank_free = [[m.sem(f"bank_free{e}{b}") for b in range(4)] for e in range(2)]
        q_level = m.sem("q_level")
        k_level = m.sem("k_level")
        sq_ready = m.sem("hsq_ready")
        red_ready = m.sem("hred_ready")
        st_step = m.sem("st_step")
        passed = m.sem("h_passed")
        og_ready = m.sem("og_ready")
        og_stored = [m.sem(f"og_stored{e}") for e in range(2)]
        n_two = GH // 4
        STEPS = 11
        MB = 4 * STEPS
        KL = 2 * (NLEV - 1)
        T_, DS_, O_ = 8, 9, 10

        def count(i, u, each, c):
            return i * (2 * each) + (u * each + c)

        def tot_at(e, j):
            if j == 0:
                return f[:, e, :]
            lo = SEQ - (SEQ >> (j - 1))
            return tot[:, e, lo:lo + (SEQ >> j)]

        def level_views(t, e, j, side):
            return t[:, e, :].rearrange("p (b s m) -> p b s m", s=2, m=1 << j)[:, :, side, :]

        def pair_tot(e, j, side):
            nb = SEQ >> (j + 1)
            one = tot_at(e, j).rearrange("p (b s) -> p b s", s=2)[:, :, side]
            return one.unsqueeze(2).to_broadcast([P, nb, 1 << j])

        with nc.Block() as block:
            @block.sync
            def _(sp):
                sp.sem_inc(og_stored[0], 16)
                sp.sem_inc(og_stored[1], 16)
                def load_qkf(i, u, first):
                    for e in range(2):
                        rows = bass.ds(i * (4 * P) + (2 * u + e) * P, P)
                        if u >= 2:
                            sp.wait_ge(mm_ready[e], count(i, u - 2, MB, MB))
                        if first:
                            sp.dma_start(k[:, e, :], scr["gf"][1][rows, :]).then_inc(k_in[e], 16)
                        sp.dma_start(q[:, 2 * (u % 2) + e, :], scr["gq"][0][rows, :]).then_inc(q_in[2 * (u % 2) + e], 16)
                        if e == 0 and not first:
                            sp.wait_ge(q_level, count(i, u - 1, 2 * NLEV, 4))
                            sp.wait_ge(k_level, count(i, u - 1, KL, 2))
                        sp.dma_start(f[:, e, :], scr["gf"][0][rows, :]).then_inc(f_in[e], 16)
                    for e in range(2):
                        if not first:
                            rows = bass.ds(i * (4 * P) + (2 * u + e) * P, P)
                            sp.wait_ge(mm_ready[e], count(i, u - 1, MB, 4 * (T_ + 1)))
                            sp.dma_start(k[:, e, :], scr["gf"][1][rows, :]).then_inc(k_in[e], 16)

                def load_vg(i, u, e, first):
                    cols = bass.ds(i * (4 * GD) + (2 * u + e) * GD, GD)
                    if not first:
                        sp.wait_ge(mm_ready[e], count(i, u - 1, MB, MB))
                    sp.dma_start(val[:, e], scr["gi"][0][:, :, cols].rearrange("b p n -> p b n")).then_inc(val_in[e], 16)
                    if not first:
                        sp.wait_ge(og_ready, count(i, u - 1, 8, 4 * (e + 1)))
                    sp.dma_start(gat[:, e], scr["gg"][0][:, :, cols].rearrange("b p n -> p b n")).then_inc(gat_in[e], 16)

                def store(i, u, e):
                    sp.wait_ge(og_ready, count(i, u, 8, 4 * (e + 1)))
                    cols = bass.ds(i * (4 * GD) + (2 * u + e) * GD, GD)
                    sp.dma_start(o_scr[:, :, cols].rearrange("b p n -> p b n"), og[:, e]).then_inc(og_stored[e], 16)

                def turn(i, u):
                    load_qkf(i, u, False)
                    for e in range(2):
                        load_vg(i, u, e, False)
                        store(i, u - 1, e)

                load_qkf(0, 0, True)
                sp.dma_start(mask[:, :, :], io["mask"]).then_inc(mask_in, 16)
                load_vg(0, 0, 0, True)
                load_vg(0, 0, 1, True)
                with nc.sync.Fori(0, n_two - 1) as i:
                    turn(i, 1)
                    turn(i, 2)
                turn(n_two - 1, 1)
                for e in range(2):
                    store(n_two - 1, 1, e)
                    sp.wait_ge(og_stored[e], 16 * (2 * n_two + 1))

            @block.tensor
            def _(pe):
                ident = keep["ident"]

                with nc.tensor.Fori(0, n_two) as i:
                    for u in range(2):
                        for s in range(STEPS):
                            for e in range(2):
                                if s == 0:
                                    pe.wait_ge(k_in[e], count(i, u, 16, 16))
                                    pe.wait_ge(q_in[2 * u + e], i * 16 + 16)
                                elif s <= NLEV:
                                    pe.wait_ge(q_level, count(i, u, 2 * NLEV, 2 * (s - 1) + e + 1))
                                    if s >= 2:
                                        pe.wait_ge(k_level, count(i, u, KL, 2 * (s - 2) + e + 1))
                                elif s == DS_:
                                    pe.wait_ge(val_in[e], count(i, u, 16, 16))
                                for b in range(4):
                                    pe.wait_ge(bank_free[e][b], count(i, u, STEPS, s + 1))
                                    for r in range(4):
                                        c = 4 * b + r
                                        out = ps[e][b][:, r * P:(r + 1) * P]
                                        toks = slice(c * P, (c + 1) * P)
                                        if s == NLEV - 1:
                                            half = slice(c * P, c * P + P // 2)
                                            last = slice(c * P + P // 2, (c + 1) * P)
                                            mm = nc.tensor.matmul(out[0:P // 2, P // 2:P], k[:, e, half], q[:, 2 * u + e, last],
                                                                  start=True, stop=True)
                                        elif s < NLEV:
                                            mm = nc.tensor.matmul(out, k[:, e, toks], q[:, 2 * u + e, toks], start=True, stop=True)
                                        elif s == T_:
                                            mm = nc.tensor.transpose(out, k[:, e, toks], ident[:, :])
                                        elif s == DS_:
                                            if c < TB - 1:
                                                mm = nc.tensor.matmul(out, kt[:, e, c, :], val[:, e, c, :], start=True, stop=True)
                                        else:
                                            mm = nc.tensor.matmul(out, sc[:, e, toks], val[:, e, c, :], start=True, stop=(c == 0))
                                            if c > 0:
                                                mm = nc.tensor.matmul(out, q[:, 2 * u + e, toks], state[:, e, c, :], start=False, stop=True)
                                    mm.then_inc(mm_ready[e], 1)

            @block.scalar
            def _(act):
                with nc.scalar.Fori(0, n_two) as i:
                    for u in range(2):
                        for s in (6, 7, T_, O_):
                            for e in range(2):
                                for b in range(4):
                                    act.wait_ge(mm_ready[e], count(i, u, MB, 4 * s + b + 1))
                                    src = ps[e][b][:, :].rearrange("p (c n) -> p c n", c=4)
                                    dst = sc[:, e, b * 512:(b + 1) * 512].rearrange("p (c n) -> p c n", c=4)
                                    if s == 6:
                                        nc.scalar.activation(dst[0:32, :, 32:64], src[0:32, :, 32:64], ACT.Copy)
                                        nc.scalar.activation(dst[64:96, :, 96:128], src[64:96, :, 96:128],
                                                             ACT.Copy).then_inc(bank_free[e][b], 1)
                                    elif s == 7:
                                        nc.scalar.activation(dst[0:64, :, 64:128], src[0:64, :, 64:128],
                                                             ACT.Copy).then_inc(bank_free[e][b], 1)
                                    elif s == T_:
                                        nc.scalar.activation(kt[:, e, 4 * b:4 * b + 4, :], src, ACT.Copy).then_inc(bank_free[e][b], 1)
                                    else:
                                        act.wait_ge(red_ready, count(i, u, 8, 4 * e + b + 1))
                                        nc.scalar.activation(sqr[:, b % 2, :], ps[e][b][:, :], ACT.Square).then_inc(sq_ready, 1)

            @block.gpsimd
            def _(pool):
                with nc.gpsimd.Fori(0, n_two) as i:
                    for u in range(2):
                        for s in range(1, NLEV):
                            for e in range(2):
                                j = s - 1
                                if j == 0:
                                    pool.wait_ge(f_in[e], count(i, u, 16, 16))
                                if j > 0:
                                    pool.wait_ge(k_level, count(i, u, KL, 2 * (s - 2) + e + 1))
                                pool.wait_ge(q_level, count(i, u, 2 * NLEV, 2 * (s - 1) + e + 1))
                                nc.gpsimd.tensor_tensor(tot_at(e, j + 1), tot_at(e, j).rearrange("p (b s) -> p b s", s=2)[:, :, 0],
                                                        tot_at(e, j).rearrange("p (b s) -> p b s", s=2)[:, :, 1], ALU.mult)
                                pool.wait_ge(mm_ready[e], count(i, u, MB, 4 * (s + 1)))
                                kk = level_views(k, e, j, 0)
                                nc.gpsimd.tensor_tensor(kk, kk, pair_tot(e, j, 1), ALU.mult).then_inc(k_level, 1)

            @block.vector
            def _(dve):
                nc.vector.memset(sc[:, 0, :], 0.0).then_inc(zeroed, 1)
                nc.vector.memset(sc[:, 1, :], 0.0).then_inc(zeroed, 1)
                nc.vector.memset(state[:, :, 0, :], 0.0).then_inc(zeroed, 1)
                for e in range(2):
                    for b in range(4):
                        nc.vector.sem_inc(bank_free[e][b], 1)
                nc.vector.sem_inc(red_ready, 2)
                dve.wait_ge(mask_in, 16)
                dve.wait_ge(zeroed, 3)
                with nc.vector.Fori(0, n_two) as i:
                    for u in range(2):
                        for s in range(NLEV):
                            for e in range(2):
                                if s < NPRED:
                                    for b in range(4):
                                        dve.wait_ge(mm_ready[e], count(i, u, MB, 4 * s + b + 1))
                                        nc.vector.sem_inc(passed, 1)
                                        dst = sc[:, e, b * 512:(b + 1) * 512].rearrange("p (c n) -> p c n", c=4)
                                        nc.vector.copy_predicated(dst, mask[:, s, :].unsqueeze(1).to_broadcast([P, 4, P]),
                                                                  ps[e][b][:, :].rearrange("p (c n) -> p c n", c=4)).then_inc(bank_free[e][b], 1)
                                else:
                                    dve.wait_ge(mm_ready[e], count(i, u, MB, 4 * (s + 1)))
                                if s == 0:
                                    dve.wait_ge(f_in[e], count(i, u, 16, 16))
                                    nc.vector.tensor_tensor(q[:, 2 * u + e, :], q[:, 2 * u + e, :], f[:, e, :], ALU.mult).then_inc(q_level, 1)
                                else:
                                    j = s - 1
                                    dve.wait_ge(q_level, count(i, u, 2 * NLEV, 2 * (s - 1) + e + 1))
                                    if j > 0:
                                        dve.wait_ge(k_level, count(i, u, KL, 2 * (s - 2) + e + 1))
                                    qq = level_views(q, 2 * u + e, j, 1)
                                    nc.vector.tensor_tensor(qq, qq, pair_tot(e, j, 0), ALU.mult).then_inc(q_level, 1)
                        for e in range(2):
                            decay = tot_at(e, 7)
                            dve.wait_ge(k_level, count(i, u, KL, KL - 1 + e))
                            for c in range(TB - 1):
                                b, r = c // 4, c % 4
                                if r == 0:
                                    dve.wait_ge(mm_ready[e], count(i, u, MB, 4 * DS_ + b + 1))
                                if c > 0:
                                    dve.wait_ge(st_step, count(i, u, 2 * (TB - 1), e * (TB - 1) + c))
                                nc.vector.scalar_tensor_tensor(state[:, e, c + 1, :], state[:, e, c, :], decay[:, c:c + 1],
                                                               ps[e][b][:, r * P:(r + 1) * P], ALU.mult, ALU.add).then_inc(st_step, 1)
                                if r == 3 or c == TB - 2:
                                    dve.wait_ge(st_step, count(i, u, 2 * (TB - 1), e * (TB - 1) + c + 1))
                                    nc.vector.sem_inc(bank_free[e][b], 1)
                        for e in range(2):
                            dve.wait_ge(gat_in[e], count(i, u, 16, 16))
                            dve.wait_ge(og_stored[e], count(i, u, 16, 16))
                            for b in range(4):
                                dve.wait_ge(sq_ready, count(i, u, 8, 4 * e + b + 1))
                                nc.vector.tensor_reduce(keep["stats"][:, bass.ds(i * (4 * TB) + ((2 * u + e) * TB + 4 * b), 4)],
                                                        sqr[:, b % 2, :].rearrange("p (c n) -> p c n", c=4), AX.X,
                                                        ALU.add).then_inc(red_ready, 1)
                                nc.vector.tensor_tensor(og[:, e, 4 * b:4 * b + 4, :], ps[e][b][:, :].rearrange("p (c n) -> p c n", c=4),
                                                        gat[:, e, 4 * b:4 * b + 4, :], ALU.mult).then_inc(og_ready, 1)
                                dve.wait_ge(og_ready, count(i, u, 8, 4 * e + b + 1))
                                nc.vector.sem_inc(bank_free[e][b], 1)


def stick(nc, io, keep, scr, o_scr):
    pieces = []
    for qb in range(TB):
        end = (qb + 1) * P
        cut = 0 if end <= D else (512 if end <= D + 512 else D)
        pieces.append((qb, cut, end - cut))
        if cut:
            pieces.append((qb, 0, cut))
    NP = len(pieces)
    PP = 2 * NP
    parts = [[(lo + a, min(512, width - a)) for a in range(0, width, 512)] for _, lo, width in pieces]
    before = [sum(len(x) for x in parts[:n]) for n in range(NP)]
    NS = sum(len(x) for x in parts)
    SS = 2 * NS
    SCALE = float(SD) ** -0.5
    with ExitStack() as stack:
        m = Mem(nc, stack)
        q = m.sb("aq", [P, 2, SEQ], F32R)
        k_hi = m.sb("ak_hi", [P, 2, SEQ], F32R)
        k_lo = m.sb("ak_lo", [P, 2, SEQ], F32R)
        val = m.sb("av", [P, 2, TB, SD])
        gat = m.sb("ag", [P, 2, TB, SD])
        beta = m.sb("beta", [P, 4, D])
        left = m.sb("left", [P, 4, D])
        run = m.sb("run", [P, 4, SEQ + 1])
        w = m.sb("w", [P, 4, D])
        wt = m.sb("wt", [P, 4, 512])
        og = m.sb("aog", [P, TB, 2, SD])
        sqr = m.sb("asqr", [P, 2, 512])
        unit_b = m.sb("unit_b", [P, P], BF16)
        never_b = m.sb("never_b", [P, P], BF16)
        never = m.sb("never", [P, P])
        z_ps = [m.ps(f"z_ps{i}", [P, D]) for i in range(2)]
        t_ps = [m.ps(f"t_ps{i}", [P, 512]) for i in range(2)]
        o_ps = [m.ps(f"o_ps{i}", [P, 512]) for i in range(2)]

        qk_in = [m.sem(f"aqk_in{e}") for e in range(2)]
        val_in = [m.sem(f"aval_in{e}") for e in range(2)]
        gat_in = [m.sem(f"agat_in{e}") for e in range(2)]
        never_in = m.sem("never_in")
        ones_set = m.sem("ones_set")
        passed = m.sem("a_passed")
        z_ready = m.sem("z_ready")
        beta_ready = m.sem("beta_ready")
        left_ready = m.sem("left_ready")
        run_ready = m.sem("run_ready")
        w_ready = m.sem("w_ready")
        t_ready = m.sem("t_ready")
        wt_ready = m.sem("wt_ready")
        av_ready = m.sem("av_ready")
        sq_ready = m.sem("asq_ready")
        red_ready = m.sem("ared_ready")
        o_free = m.sem("o_free")
        og_stored = m.sem("aog_stored")
        n_it = SH // 2
        LAG_T, LAG_AV, LAG_SQ, LAG_OUT = 3, 4, 5, 6
        half_end = [max(n for n in range(NP) if pieces[n][0] // 8 == h) for h in range(2)]

        def at(n):
            return (n // NP % 2,) + pieces[n % NP]

        def part_list(n):
            return [(n // NP * NS + before[n % NP] + a,) + x for a, x in enumerate(parts[n % NP])]

        def half_done(n):
            return half_end.index(n % NP) if n % NP in half_end else None

        def sweep(eng, step):
            for n in range(LAG_OUT):
                step(0, n, False)
            with eng.Fori(0, n_it - 1) as i:
                for n in range(LAG_OUT, PP + LAG_OUT):
                    step(i, n, False)
            for n in range(LAG_OUT, PP + LAG_OUT):
                step(n_it - 1, n, True)

        def there(n, last):
            return 0 <= n and not (last and n >= PP)

        with nc.Block() as block:
            @block.sync
            def _(sp):
                def load(i, e, first):
                    if not first:
                        sp.wait_ge(av_ready, (i - 1) * PP + NP * (e + 1))
                        sp.wait_ge(o_free, (i - 1) * 4 + (2 * (e + 1) + 2))
                    hd = i * 2 + e
                    rows = bass.ds(hd * SD, SD)
                    for dst, half, src in ((q, 0, scr["sq"][0]), (q, 1, scr["sq"][1]), (k_hi, 0, scr["sk"][0]),
                                           (k_hi, 1, scr["sk"][0]), (k_lo, 0, scr["sk"][1]), (k_lo, 1, scr["sk"][1])):
                        sp.dma_start(dst[half * SD:(half + 1) * SD, e, :].bitcast(F32), src[rows, :]).then_inc(qk_in[e], 16)
                    sp.dma_start(val[:, e], scr["sv"][0][:, :, rows].rearrange("b p n -> p b n")).then_inc(val_in[e], 16)
                    sp.dma_start(gat[:, e], scr["sg"][0][:, :, rows].rearrange("b p n -> p b n")).then_inc(gat_in[e], 16)

                def store(i):
                    sp.wait_ge(o_free, i * 4 + 6)
                    cols = bass.ds(i * (2 * SD) + D, 2 * SD)
                    sp.dma_start(o_scr[:, :, cols].rearrange("b p n -> p b n"), og[:, :].rearrange("p b e n -> p b (e n)")).then_inc(og_stored, 16)

                sp.sem_inc(og_stored, 16)
                sp.dma_start(never[:, :], io["never"]).then_inc(never_in, 16)
                load(0, 0, True)
                load(0, 1, True)
                with nc.sync.Fori(0, n_it - 1) as j:
                    load(j + 1, 0, False)
                    store(j)
                    load(j + 1, 1, False)
                store(n_it - 1)
                sp.wait_ge(og_stored, 16 * n_it + 16)

            @block.tensor
            def _(pe):
                pe.wait_ge(ones_set, 3)

                def step(i, n, last):
                    if there(n, last):
                        e, qb, lo, width = at(n)
                        if n % NP == 0:
                            pe.wait_ge(qk_in[e], i * 96 + (96 if n < PP else 192))
                        pe.wait_ge(beta_ready, i * PP + (n + 1))
                        for a in range(0, width, 512):
                            wd = min(512, width - a)
                            diag = lo + a + wd == (qb + 1) * P
                            qq = q[:, e, qb * P:(qb + 1) * P]
                            zz = z_ps[n % 2][:, a:a + wd]
                            nc.tensor.matmul(zz, qq, k_hi[:, e, lo + a:lo + a + wd], start=True, stop=False)
                            if diag:
                                nc.tensor.matmul(z_ps[n % 2][:, a + wd - P:a + wd], unit_b[:, :], never_b[:, :],
                                                 start=False, stop=False, skip_group_check=True)
                            mm = nc.tensor.matmul(zz, qq, k_lo[:, e, lo + a:lo + a + wd], start=False, stop=True)
                        mm.then_inc(z_ready, 1)
                    n1 = n - LAG_T
                    if there(n1, last):
                        pe.wait_ge(w_ready, i * PP + (n1 + 1))
                        for a, key, wd in part_list(n1):
                            if a >= 2:
                                pe.wait_ge(wt_ready, i * SS + (a - 1))
                            c0 = key - at(n1)[2]
                            for j in range(wd // P):
                                mm = nc.tensor.transpose(t_ps[a % 2][:, j * P:(j + 1) * P], w[:, n1 % 4, c0 + j * P:c0 + (j + 1) * P],
                                                         keep["ident"][:, :])
                            mm.then_inc(t_ready, 1)
                    n2 = n - LAG_AV
                    if there(n2, last):
                        e, qb, lo, width = at(n2)
                        if lo + width == (qb + 1) * P and qb % 8 == 0:
                            pe.wait_ge(o_free, i * 4 + (2 * e + qb // 8 + 1 + (4 if n2 >= PP else 0)))
                        if n2 % NP == 0:
                            pe.wait_ge(val_in[e], i * 16 + (16 if n2 < PP else 32))
                        out = o_ps[qb // 8][:, (qb % 8) * SD:(qb % 8 + 1) * SD]
                        for a, key, wd in part_list(n2):
                            pe.wait_ge(wt_ready, i * SS + (a + 1))
                            for j in range(wd // P):
                                mm = nc.tensor.matmul(out, wt[:, a % 4, j * P:(j + 1) * P], val[:, e, key // P + j, :],
                                                      start=(lo + width == (qb + 1) * P and key == lo and j == 0),
                                                      stop=(lo == 0 and key + (j + 1) * P == width))
                        mm.then_inc(av_ready, 1)

                sweep(nc.tensor, step)

            @block.scalar
            def _(act):
                nc.scalar.sem_inc(beta_ready, 2)

                def step(i, n, last):
                    if there(n, last):
                        width = at(n)[3]
                        act.wait_ge(z_ready, i * PP + (n + 1))
                        nc.scalar.activation(beta[:, n % 4, 0:width], z_ps[n % 2][:, 0:width], ACT.Sigmoid,
                                             scale=SCALE).then_inc(beta_ready, 1)
                    n1 = n - LAG_T
                    if there(n1, last):
                        for a, key, wd in part_list(n1):
                            act.wait_ge(t_ready, i * SS + (a + 1))
                            nc.scalar.activation(wt[:, a % 4, 0:wd], t_ps[a % 2][:, 0:wd], ACT.Copy).then_inc(wt_ready, 1)
                    n2 = n - LAG_SQ
                    if there(n2, last) and half_done(n2) is not None:
                        h, idx = half_done(n2), 2 * (n2 // NP) + half_done(n2)
                        act.wait_ge(av_ready, i * PP + (n2 + 1))
                        act.wait_ge(red_ready, i * 4 + (idx + 1))
                        nc.scalar.activation(sqr[:, h, :], o_ps[h][:, :], ACT.Square).then_inc(sq_ready, 1)

                sweep(nc.scalar, step)

            @block.gpsimd
            def _(pool):
                def step(i, n, last):
                    if there(n, last):
                        width = at(n)[3]
                        pool.wait_ge(beta_ready, i * PP + (n + 1 + 2))
                        nc.gpsimd.sem_inc(passed, 1)
                        nc.gpsimd.tensor_scalar(left[:, n % 4, 0:width], beta[:, n % 4, 0:width], -1.0, 1.0,
                                                ALU.mult, ALU.add).then_inc(left_ready, 1)

                sweep(nc.gpsimd, step)

            @block.vector
            def _(dve):
                nc.vector.sem_inc(red_ready, 2)
                nc.vector.sem_inc(o_free, 2)
                nc.vector.memset(run[:, :, SEQ:SEQ + 1], 1.0).then_inc(ones_set, 1)
                dve.wait_ge(never_in, 16)
                nc.vector.tensor_copy(never_b[:, :], never[:, :]).then_inc(ones_set, 1)
                nc.vector.tensor_copy(unit_b[:, :], keep["ident"][:, :]).then_inc(ones_set, 1)
                dve.wait_ge(ones_set, 3)

                def place(n):
                    e, qb, lo, width = at(n)
                    return qb % 4, SEQ - (qb + 1) * P + lo, width

                def step(i, n, last):
                    if there(n, last):
                        u, lo, width = place(n)
                        dve.wait_ge(left_ready, i * PP + (n + 1))
                        if n > 0:
                            dve.wait_ge(run_ready, i * PP + n)
                        nc.vector.tensor_tensor_scan(run[:, u, lo:lo + width][:, ::-1], left[:, n % 4, 0:width][:, ::-1],
                                                     left[:, n % 4, 0:width], run[:, u, lo + width:lo + width + 1],
                                                     ALU.mult, ALU.bypass).then_inc(run_ready, 1)
                    n1 = n - 1
                    if there(n1, last):
                        u, lo, width = place(n1)
                        if not there(n, last):
                            dve.wait_ge(run_ready, i * PP + n)
                        nc.vector.tensor_tensor(w[:, n1 % 4, 0:width], beta[:, n1 % 4, 0:width],
                                                run[:, u, lo + 1:lo + width + 1], ALU.mult).then_inc(w_ready, 1)
                    n2 = n - LAG_OUT
                    if there(n2, last) and half_done(n2) is not None:
                        h, e, nxt = half_done(n2), n2 // NP % 2, n2 // PP
                        idx = 2 * (n2 // NP) + h
                        dve.wait_ge(sq_ready, i * 4 + (idx + 1))
                        nc.vector.tensor_reduce(keep["stats"][:, bass.ds(i * (2 * TB) + ((GH + e + 2 * nxt) * TB + 8 * h), 8)],
                                                sqr[:, h, :].rearrange("p (b n) -> p b n", n=SD), AX.X, ALU.add).then_inc(red_ready, 1)
                        if h == 0:
                            dve.wait_ge(gat_in[e], i * 16 + 16 * (nxt + 1))
                        dve.wait_ge(og_stored, i * 16 + 16 * nxt + 16)
                        nc.vector.tensor_tensor(og[:, 8 * h:8 * h + 8, e, :], o_ps[h][:, :].rearrange("p (b n) -> p b n", n=SD),
                                                gat[:, e, 8 * h:8 * h + 8, :], ALU.mult).then_inc(o_free, 1)

                sweep(nc.vector, step)


def output(nc, io, keep, o_scr, out):
    with ExitStack() as stack:
        m = Mem(nc, stack)
        w_hi = m.sb("wo_hi", [P, KO, D], F32R)
        w_lo = m.sb("wo_lo", [P, KO, D], F32R)
        o = m.sb("o", [P, 2, 2 * D])
        ot_hi = m.sb("ot_hi", [P, 2, 4, 512], F32R)
        ot_lo = m.sb("ot_lo", [P, 2, 4, 512], F32R)
        w_raw = m.sb("wo_raw", [P, 4, D])
        x, gy = w_raw[:, 0:2, :], w_raw[:, 2:4, :]
        g_out = m.sb("g_out", [P, D])
        rv = m.sb("rv", [P, 3, NHEAD * TB])
        fin = m.sb("fin", [P, 5])
        t_ps = [m.ps(f"ot_ps{i}", [P, 512]) for i in range(4)]
        y_ps = [m.ps(f"y_ps{i}", [P, D]) for i in range(2)]

        w_loaded = [m.sem(f"wo_loaded{k}") for k in range(KO)]
        w_high = m.sem("wo_high")
        w_split = m.sem("wo_split")
        g_in = m.sem("g_in")
        o_in = [m.sem(f"o_in{i}") for i in range(2)]
        x_in = [m.sem(f"ox_in{i}") for i in range(2)]
        root_in = m.sem("root_in")
        root_ready = m.sem("oroot_ready")
        r_step = m.sem("r_step")
        on_ready = m.sem("on_ready")
        t_ready = m.sem("ot_ready")
        hi_ready = m.sem("ohi_ready")
        lo_ready = m.sem("olo_ready")
        y_ready = m.sem("y_ready")
        y_taken = m.sem("y_taken")
        y_step = m.sem("y_step")
        sum_ready = m.sem("sum_ready")
        var_ready = m.sem("ovar_ready")
        froot_ready = m.sem("froot_ready")
        out_ready = m.sem("out_ready")
        out_stored = [m.sem(f"out_stored{i}") for i in range(2)]
        YS = 8
        n_loop = TB // 2 - 2

        with nc.Block() as block:
            @block.sync
            def _(sp):
                def load_o(i, t):
                    if t >= 2:
                        sp.wait_ge(t_ready, i * 8 + 4 * (t - 1))
                    sp.dma_start(o[:, t % 2, :], o_scr[bass.ds(i * 2 + t, 1)].rearrange("a p n -> p (a n)")).then_inc(o_in[t % 2], 16)

                def load_x(i, t):
                    if t >= 2:
                        sp.wait_ge(out_stored[t % 2], i * 16 + 16 * (t // 2))
                    sp.dma_start(x[:, t % 2, :], io["x_blocks"][bass.ds(i * 2 + t, 1)].rearrange("a p n -> p (a n)")).then_inc(x_in[t % 2], 16)

                def load_w(k):
                    if k >= 4:
                        sp.wait_ge(w_split, k - 3)
                    sp.dma_start(w_raw[:, k % 4, :], io["w_out"][:, k, :]).then_inc(w_loaded[k], 16)

                def store(i, t):
                    sp.wait_ge(out_ready, i * 2 + (t + 1))
                    sp.dma_start(out[bass.ds(i * 2 + t, 1)].rearrange("a p n -> p (a n)"), x[:, t % 2, :]).then_inc(out_stored[t % 2], 16)

                load_o(0, 0)
                load_o(0, 1)
                for k in range(KO):
                    load_w(k)
                sp.dma_start(g_out[:, :], io["final_g"].partition_broadcast(P)).then_inc(g_in, 16)
                load_o(0, 2)
                load_o(0, 3)
                sp.wait_ge(w_split, KO)
                load_x(0, 0)
                load_x(0, 1)
                store(0, 0)
                load_x(0, 2)
                with nc.sync.Fori(0, n_loop) as i:
                    for t in (2, 3):
                        load_o(i, t + 2)
                        store(i, t - 1)
                        load_x(i, t + 1)
                store(n_loop, 1)
                load_x(n_loop, 3)
                store(n_loop, 2)
                store(n_loop, 3)
                for e in range(2):
                    sp.wait_ge(out_stored[e], 16 * (TB // 2))

            @block.tensor
            def _(pe):
                def transposes(i, t):
                    pe.wait_ge(on_ready, i * 4 + 2 * (t + 1))
                    for b in range(4):
                        if t >= 1:
                            pe.wait_ge(lo_ready, i * 8 + (4 * (t - 1) + b + 1))
                        for r in range(4):
                            j = 4 * b + r
                            mm = nc.tensor.transpose(t_ps[b][:, r * P:(r + 1) * P], o[:, t % 2, j * P:(j + 1) * P], keep["ident"][:, :])
                        mm.then_inc(t_ready, 1)

                def product(t, k, h, ot, wt, start, stop):
                    return nc.tensor.matmul(y_ps[t % 2][:, h * 512:(h + 1) * 512], ot[:, t % 2, k // 4, (k % 4) * P:(k % 4 + 1) * P],
                                            wt[:, k, h * 512:(h + 1) * 512], start=start, stop=stop)

                def products(i, t):
                    pe.wait_ge(y_taken, i * 2 + (t - 1))
                    for h in range(2):
                        for j, (ot, wt) in enumerate(((ot_hi, w_hi), (ot_lo, w_hi), (ot_hi, w_lo))):
                            for k in range(KO):
                                mm = product(t, k, h, ot, wt, j == 0 and k == 0, j == 2 and k == KO - 1)
                    mm.then_inc(y_ready, 1)

                transposes(0, 0)
                transposes(0, 1)
                pe.wait_ge(lo_ready, 8)
                for k in range(KO):
                    pe.wait_ge(w_split, k + 1)
                    for t in range(2):
                        for h in range(2):
                            product(t, k, h, ot_hi, w_hi, k == 0, False)
                            product(t, k, h, ot_lo, w_hi, False, False)
                            mm = product(t, k, h, ot_hi, w_lo, False, k == KO - 1)
                        if k == KO - 1:
                            mm.then_inc(y_ready, 1)
                transposes(0, 2)
                with nc.tensor.Fori(0, n_loop) as i:
                    for t in (2, 3):
                        transposes(i, t + 1)
                        products(i, t)
                transposes(n_loop, 3)
                products(n_loop, 2)
                pe.wait_ge(lo_ready, 4 * TB)
                products(n_loop, 3)

            @block.scalar
            def _(act):
                act.wait_ge(root_in, 1)
                nc.scalar.activation(rv[:, 1, :], rv[:, 0, :], ACT.Sqrt).then_inc(root_ready, 1)

                def split(i, t):
                    if t >= 2:
                        act.wait_ge(y_ready, i * 2 + (t - 1))
                    for b in range(4):
                        act.wait_ge(t_ready, i * 8 + (4 * t + b + 1))
                        nc.scalar.activation(ot_hi[:, t % 2, b, :], t_ps[b][:, :], ACT.Copy).then_inc(hi_ready, 1)

                def final(i, t):
                    act.wait_ge(y_step, i * (2 * YS) + (t * YS + 3))
                    nc.scalar.activation(gy[:, t % 2, :], x[:, t % 2, :], ACT.Square, accum_out=fin[:, 0:1]).then_inc(sum_ready, 1)
                    act.wait_ge(var_ready, i * 2 + (t + 1))
                    nc.scalar.activation(fin[:, 2:3], fin[:, 1:2], ACT.Sqrt).then_inc(froot_ready, 1)

                split(0, 0)
                split(0, 1)
                for k in range(KO):
                    act.wait_ge(w_loaded[k], 16)
                    nc.scalar.activation(w_hi[:, k, :], w_raw[:, k % 4, :], ACT.Copy).then_inc(w_high, 1)
                split(0, 2)
                final(0, 0)
                final(0, 1)
                with nc.scalar.Fori(0, n_loop) as i:
                    for t in (2, 3):
                        split(i, t + 1)
                        final(i, t)
                split(n_loop, 3)
                final(n_loop, 2)
                final(n_loop, 3)

            @block.vector
            def _(dve):
                n_g = GH * TB
                n_all = NHEAD * TB
                var, root, a = (rv[:, j, :] for j in range(3))
                stats = keep["stats"]
                r = keep["stats"][:, :]
                nc.vector.tensor_scalar(rv[:, 0, 0:n_g], stats[:, 0:n_g], 1.0 / GD, EPS, ALU.mult, ALU.add).then_inc(r_step, 1)
                nc.vector.tensor_scalar(rv[:, 0, n_g:n_all], stats[:, n_g:n_all], 1.0 / SD, EPS, ALU.mult, ALU.add).then_inc(root_in, 1)
                dve.wait_ge(r_step, 1)
                dve.wait_ge(root_ready, 1)
                nc.vector.reciprocal(r, root).then_inc(r_step, 1)
                dve.wait_ge(r_step, 2)
                nc.vector.tensor_tensor(a, r, r, ALU.mult).then_inc(r_step, 1)
                dve.wait_ge(r_step, 3)
                nc.vector.tensor_tensor(a, a, var, ALU.mult).then_inc(r_step, 1)
                dve.wait_ge(r_step, 4)
                nc.vector.tensor_scalar(a, a, -0.5, 1.5, ALU.mult, ALU.add).then_inc(r_step, 1)
                dve.wait_ge(r_step, 5)
                nc.vector.tensor_tensor(r, r, a, ALU.mult).then_inc(r_step, 1)
                dve.wait_ge(r_step, 6)

                def head_norm(i, t):
                    dve.wait_ge(o_in[t % 2], i * 16 + 16 * (t // 2 + 1))
                    rr = r.rearrange("p (h t) -> p h t", t=TB)[:, :, bass.ds(i * 2 + t, 1)]
                    for lo, h0, nh, dh in ((0, 0, GH, GD), (D, GH, SH, SD)):
                        v = o[:, t % 2, lo:lo + D].rearrange("p (h n) -> p h n", n=dh)
                        nc.vector.tensor_tensor(v, v, rr[:, h0:h0 + nh, :].to_broadcast([P, nh, dh]), ALU.mult).then_inc(on_ready, 1)

                def split(i, t):
                    for b in range(4):
                        dve.wait_ge(hi_ready, i * 8 + (4 * t + b + 1))
                        nc.vector.tensor_tensor(ot_lo[:, t % 2, b, :], t_ps[b][:, :], ot_hi[:, t % 2, b, :].bitcast(F32),
                                                ALU.subtract).then_inc(lo_ready, 1)

                def final(i, t):
                    e = t % 2
                    at = [i * (2 * YS) + t * YS, 0]

                    def done(ins):
                        at[1] += 1
                        ins.then_inc(y_step, 1)
                        dve.wait_ge(y_step, at[0] + at[1])

                    dve.wait_ge(y_ready, i * 2 + (t + 1))
                    done(nc.vector.tensor_tensor(gy[:, e, 0:512], y_ps[e][:, 0:512], keep["gate"][:, 0:512], ALU.mult))
                    nc.vector.tensor_tensor(gy[:, e, 512:D], y_ps[e][:, 512:D], keep["gate"][:, 512:D], ALU.mult).then_inc(y_taken, 1)
                    dve.wait_ge(y_taken, i * 2 + (t + 1))
                    dve.wait_ge(x_in[e], i * 16 + 16 * (t // 2 + 1))
                    done(nc.vector.tensor_tensor(x[:, e, 0:512], x[:, e, 0:512], gy[:, e, 0:512], ALU.add))
                    done(nc.vector.tensor_tensor(x[:, e, 512:D], x[:, e, 512:D], gy[:, e, 512:D], ALU.add))
                    dve.wait_ge(sum_ready, i * 2 + (t + 1))
                    nc.vector.tensor_scalar(fin[:, 1:2], fin[:, 0:1], 1.0 / D, EPS, ALU.mult, ALU.add).then_inc(var_ready, 1)
                    dve.wait_ge(froot_ready, i * 2 + (t + 1))
                    done(nc.vector.reciprocal(fin[:, 3:4], fin[:, 2:3]))
                    done(nc.vector.tensor_tensor(fin[:, 4:5], fin[:, 3:4], fin[:, 3:4], ALU.mult))
                    done(nc.vector.tensor_tensor(fin[:, 4:5], fin[:, 4:5], fin[:, 1:2], ALU.mult))
                    done(nc.vector.tensor_scalar(fin[:, 4:5], fin[:, 4:5], -0.5, 1.5, ALU.mult, ALU.add))
                    done(nc.vector.tensor_tensor(fin[:, 3:4], fin[:, 3:4], fin[:, 4:5], ALU.mult))
                    nc.vector.scalar_tensor_tensor(x[:, e, :], x[:, e, :], fin[:, 3:4], g_out[:, :],
                                                   ALU.mult, ALU.mult).then_inc(out_ready, 1)

                head_norm(0, 0)
                head_norm(0, 1)
                split(0, 0)
                split(0, 1)
                for k in range(KO):
                    dve.wait_ge(w_high, k + 1)
                    nc.vector.tensor_tensor(w_lo[:, k, :], w_raw[:, k % 4, :], w_hi[:, k, :].bitcast(F32),
                                            ALU.subtract).then_inc(w_split, 1)
                head_norm(0, 2)
                split(0, 2)
                head_norm(0, 3)
                dve.wait_ge(g_in, 16)
                final(0, 0)
                final(0, 1)
                with nc.vector.Fori(0, n_loop) as i:
                    for t in (2, 3):
                        split(i, t + 1)
                        head_norm(i, t + 2)
                        final(i, t)
                split(n_loop, 3)
                final(n_loop, 2)
                final(n_loop, 3)


def build(nc, io, out):
    scr = {
        "gq": [nc.dram_tensor("s_gq", (D, SEQ), F32).ap()],
        "gf": [nc.dram_tensor(f"s_g{n}", (D, SEQ), F32).ap() for n in "fk"],
        "sq": [nc.dram_tensor(f"s_q{n}", (D, SEQ), F32).ap() for n in ("hi", "lo")],
        "sk": [nc.dram_tensor(f"s_k{n}", (D, SEQ), F32).ap() for n in ("hi", "lo")],
    }
    for name in ("gi", "gg", "sv", "sg"):
        scr[name] = [nc.dram_tensor(f"s_{name}", (TB, P, D), F32).ap()]
    o_scr = nc.dram_tensor("s_o", (TB, P, 2 * D), F32).ap()
    with ExitStack() as stack:
        m = Mem(nc, stack)
        keep = {
            "ident": m.sb("ident", [P, P]),
            "gate": m.sb("gate", [P, D]),
            "lb": m.sb("lb", [P, 2, GH]),
            "g_hgrn": m.sb("g_hgrn", [P, GD]),
            "g_stick": m.sb("g_stick", [P, SD]),
            "stats": m.sb("stats", [P, NHEAD * TB]),
        }
        with ExitStack() as hstack:
            hm = Mem(nc, hstack)
            h_hi = hm.sb("h_hi", [P, KD, SEQ], F32R)
            h_lo = hm.sb("h_lo", [P, KD, SEQ], F32R)
            w_raw = hm.sb("w_raw", [P, KD, WC])
            w_first = hm.sem("w_first")
            condition(nc, io, keep, h_hi, h_lo, w_raw, w_first)
            project(nc, io, keep, h_hi, h_lo, w_raw, w_first, scr)
        hgrn(nc, io, keep, scr, o_scr)
        stick(nc, io, keep, scr, o_scr)
        output(nc, io, keep, o_scr, out)


def level_masks(np):
    s, t = np.arange(P)[:, None], np.arange(P)[None, :]
    masks = [s == t]
    for j in range(NPRED - 1):
        b = 1 << j
        masks.append((t // b == s // b + 1) & (s // b % 2 == 0))
    return np.stack(masks, 1).astype(np.int32)


def never_mask(np):
    return np.where(np.arange(P)[None, :] < np.arange(P)[:, None], 0.0, -1e30).astype(np.float32)


def kernel(x, c, w_ada, b_ada, norm_g, w_in, lb_logits, hgrn_norm_g, sb_norm_g, w_out, final_g):
    import numpy as np
    import concourse.bacc as bacc
    from concourse.bass_utils import run_bass_kernel_spmd

    def col(v):
        return np.asarray(v).reshape(KD, P).T

    x = np.asarray(x)[0]
    b_ada = np.asarray(b_ada)[0]
    w_in = np.asarray(w_in)[0].reshape(KD, P, 8, CH_T, WC)
    w_in = w_in[:, :, [p[2] for p in PROJ]]
    arrays = {
        "x": x,
        "small": np.stack([col(c), col(b_ada[:D]), col(b_ada[D:2 * D]), col(norm_g), col(lb_logits)], 1),
        "b_gate": b_ada[2 * D:],
        "w_ada": np.asarray(w_ada)[0].reshape(KD, P, 12, 256).transpose(2, 1, 0, 3),
        "w_in": w_in.transpose(2, 3, 1, 0, 4).reshape(NCH, P, KD, WC),
        "w_out": np.asarray(w_out)[0].reshape(KO, P, D).transpose(1, 0, 2),
        "g_hgrn": np.asarray(hgrn_norm_g)[0],
        "g_stick": np.asarray(sb_norm_g)[0],
        "final_g": np.asarray(final_g),
        "ident": np.eye(P, dtype=np.float32),
        "mask": level_masks(np),
        "never": never_mask(np),
    }
    nc = bacc.Bacc("TRN2", target_bir_lowering=False, num_devices=1)
    io, ins = {}, {}
    for name, a in arrays.items():
        a = np.ascontiguousarray(a)
        ins[f"in_{name}"] = a
        io[name] = nc.dram_tensor(f"in_{name}", a.shape, mybir.dt.from_np(a.dtype), kind="ExternalInput").ap()
    io["x_blocks"] = io["x"].rearrange("(b p) n -> b p n", p=P)
    out = nc.dram_tensor("out", (TB, P, D), F32, kind="ExternalOutput").ap()
    build(nc, io, out)
    r = run_bass_kernel_spmd(nc, [ins], core_ids=[0])
    return r.results[0]["out"].reshape(1, SEQ, D)
```
